# Optimizing a Trainium2 kernel written in Bass

```python
import math
import jax
import jax.numpy as jnp
from jax import lax
import numpy as np

D_MODEL = 2048
BATCH = 1
SEQ = 256
DEPTH = 1

SSD_EXPAND = 2
SSD_D_INNER = SSD_EXPAND * D_MODEL
SSD_HEAD_DIM = 64
SSD_N_HEADS = SSD_D_INNER // SSD_HEAD_DIM
SSD_N_GROUPS = 8
SSD_D_STATE = 128
SSD_CONV_WIDTH = 4
SSD_CHUNK = 128
SSD_XBC = SSD_D_INNER + 2 * SSD_N_GROUPS * SSD_D_STATE

ATTN_HEAD_DIM = 64
ATTN_N_Q_HEADS = D_MODEL // ATTN_HEAD_DIM
ATTN_N_KV_HEADS = ATTN_N_Q_HEADS // 8
ATTN_Q_WIDTH = ATTN_N_Q_HEADS * ATTN_HEAD_DIM
ATTN_KV_WIDTH = ATTN_N_KV_HEADS * ATTN_HEAD_DIM
ATTN_WINDOW = 128
ROPE_THETA = 10000.0

FFN_HIDDEN = 5632

DEEPNORM_ALPHA = (2 * DEPTH) ** 0.25
DEEPNORM_BETA = (8 * DEPTH) ** -0.25
LN_EPS = 1e-5
RMS_EPS = 1e-5

PROJ_SIZES = (SSD_D_INNER, SSD_XBC, SSD_N_HEADS, ATTN_Q_WIDTH, ATTN_KV_WIDTH, ATTN_KV_WIDTH, D_MODEL, D_MODEL)
PROJ_SPLITS = tuple(int(s) for s in np.cumsum(PROJ_SIZES)[:-1])
PROJ_WIDTH = int(sum(PROJ_SIZES))

kernel_name = 'hybrid_ssd_swa_sink_macaron_deepnorm'

def layer_norm(x, g, b):
    xf = x.astype(jnp.float32)
    mu = jnp.mean(xf, axis=-1, keepdims=True)
    xc = xf - mu
    var = jnp.mean(xc * xc, axis=-1, keepdims=True)
    return (xc * lax.rsqrt(var + LN_EPS) * g + b).astype(x.dtype)

def swiglu(x, w_gate, w_up, w_down):
    return (jax.nn.silu(x @ w_gate) * (x @ w_up)) @ w_down

def causal_depthwise_conv(u, w, b):
    k_width, ch = w.shape
    y = lax.conv_general_dilated(
        u, w[:, None, :], window_strides=(1,), padding=[(k_width - 1, 0)],
        dimension_numbers=('NWC', 'WIO', 'NWC'), feature_group_count=ch)
    return y + b

def ssd_chunked(x, dt, a, bmat, cmat):
    bsz, t_len, n_heads, p_dim = x.shape
    n_groups, n_state = bmat.shape[2], bmat.shape[3]
    r = n_heads // n_groups
    q_len = SSD_CHUNK
    n_chunks = t_len // q_len
    xd = (x * dt[..., None]).reshape(bsz, n_chunks, q_len, n_groups, r, p_dim)
    adt = (dt * a).reshape(bsz, n_chunks, q_len, n_groups, r).transpose(0, 1, 3, 4, 2)
    bc = bmat.reshape(bsz, n_chunks, q_len, n_groups, n_state)
    cc = cmat.reshape(bsz, n_chunks, q_len, n_groups, n_state)
    a_cs = jnp.cumsum(adt, axis=-1)
    causal = jnp.tril(jnp.ones((q_len, q_len), dtype=bool))
    seg = jnp.exp(jnp.where(causal, a_cs[..., :, None] - a_cs[..., None, :], -jnp.inf))
    cb = jnp.einsum('bclgn,bcsgn->bcgls', cc, bc)
    y_diag = jnp.einsum('bcgrls,bcsgrp->bclgrp', cb[:, :, :, None] * seg, xd)
    decay_to_end = jnp.exp(a_cs[..., -1:] - a_cs).transpose(0, 1, 4, 2, 3)
    states = jnp.einsum('bclgn,bclgrp->bcgrpn', bc, xd * decay_to_end[..., None])
    chunk_decay = jnp.exp(a_cs[..., -1])

    def step(h, inp):
        s_c, d_c = inp
        return h * d_c[..., None, None] + s_c, h

    h0 = jnp.zeros((bsz, n_groups, r, p_dim, n_state), dtype=states.dtype)
    _, prev = lax.scan(step, h0, (jnp.moveaxis(states, 1, 0), jnp.moveaxis(chunk_decay, 1, 0)))
    prev = jnp.moveaxis(prev, 0, 1)
    decay_in = jnp.exp(a_cs).transpose(0, 1, 4, 2, 3)
    y_off = jnp.einsum('bclgn,bcgrpn->bclgrp', cc, prev) * decay_in[..., None]
    return (y_diag + y_off).reshape(bsz, t_len, n_heads, p_dim)

def ssd_branch(z, xbc, dt_raw, conv_w, conv_b, dt_bias, a_log, d_skip, norm_g, w_o):
    bsz, t_len, _ = z.shape
    xbc = jax.nn.silu(causal_depthwise_conv(xbc, conv_w, conv_b))
    gn = SSD_N_GROUPS * SSD_D_STATE
    xs = xbc[..., :SSD_D_INNER].reshape(bsz, t_len, SSD_N_HEADS, SSD_HEAD_DIM).astype(jnp.float32)
    bm = xbc[..., SSD_D_INNER:SSD_D_INNER + gn].reshape(bsz, t_len, SSD_N_GROUPS, SSD_D_STATE).astype(jnp.float32)
    cm = xbc[..., SSD_D_INNER + gn:].reshape(bsz, t_len, SSD_N_GROUPS, SSD_D_STATE).astype(jnp.float32)
    dt = jax.nn.softplus(dt_raw.astype(jnp.float32) + dt_bias.astype(jnp.float32))
    a = -jnp.exp(a_log.astype(jnp.float32))
    y = ssd_chunked(xs, dt, a, bm, cm) + d_skip.astype(jnp.float32)[:, None] * xs
    y = y.reshape(bsz, t_len, SSD_D_INNER) * jax.nn.silu(z.astype(jnp.float32))
    yg = y.reshape(bsz, t_len, SSD_N_GROUPS, SSD_D_INNER // SSD_N_GROUPS)
    yg = yg * lax.rsqrt(jnp.mean(yg * yg, axis=-1, keepdims=True) + RMS_EPS)
    y = yg.reshape(bsz, t_len, SSD_D_INNER) * norm_g.astype(jnp.float32)
    return y.astype(z.dtype) @ w_o

def rope(u, positions):
    dh = u.shape[-1]
    half = dh // 2
    inv_freq = ROPE_THETA ** (-jnp.arange(half, dtype=jnp.float32) * 2.0 / dh)
    ang = positions.astype(jnp.float32)[..., None] * inv_freq
    cos = jnp.cos(ang)[:, :, None, :]
    sin = jnp.sin(ang)[:, :, None, :]
    uf = u.astype(jnp.float32)
    u1, u2 = uf[..., :half], uf[..., half:]
    return jnp.concatenate([u1 * cos - u2 * sin, u2 * cos + u1 * sin], axis=-1).astype(u.dtype)

def sliding_window_attention(q, k, v, sinks):
    bsz, t_len, hq, dh = q.shape
    hkv = k.shape[2]
    g = hq // hkv
    w = ATTN_WINDOW
    nb = t_len // w
    qb = q.reshape(bsz, nb, w, hkv, g, dh).astype(jnp.float32)
    kb = k.reshape(bsz, nb, w, hkv, dh).astype(jnp.float32)
    vb = v.reshape(bsz, nb, w, hkv, dh).astype(jnp.float32)

    def with_prev(u):
        prev = jnp.pad(u[:, :-1], ((0, 0), (1, 0), (0, 0), (0, 0), (0, 0)))
        return jnp.concatenate([prev, u], axis=2)

    kk = with_prev(kb)
    vv = with_prev(vb)
    s = jnp.einsum('bnqhgd,bnkhd->bnhgqk', qb, kk) * (dh ** -0.5)
    qi = jnp.arange(w)[:, None]
    kj = jnp.arange(2 * w)[None, :]
    band = (kj > qi) & (kj <= qi + w)
    valid_prev = (jnp.arange(nb)[:, None, None] > 0) | (kj >= w)[None]
    mask = band[None] & valid_prev
    s = jnp.where(mask[None, :, None, None], s, -jnp.inf)
    sink = sinks.astype(jnp.float32).reshape(hkv, g)[None, None, :, :, None, None]
    m = jnp.maximum(jnp.max(s, axis=-1, keepdims=True), sink)
    p = jnp.exp(s - m)
    denom = jnp.sum(p, axis=-1, keepdims=True) + jnp.exp(sink - m)
    o = jnp.einsum('bnhgqk,bnkhd->bnqhgd', p / denom, vv)
    return o.reshape(bsz, t_len, hq * dh).astype(q.dtype)

def hybrid_mixer(h, positions, w_in, conv_w, conv_b, dt_bias, a_log, d_skip, ssd_norm_g,
                 w_ssd_o, attn_sinks, w_attn_o, w_out):
    bsz, t_len, _ = h.shape
    proj = h @ w_in
    z, xbc, dt_raw, q, k, v, gate_s, gate_a = jnp.split(proj, PROJ_SPLITS, axis=-1)
    y_s = ssd_branch(z, xbc, dt_raw, conv_w, conv_b, dt_bias, a_log, d_skip, ssd_norm_g, w_ssd_o)
    q = rope(q.reshape(bsz, t_len, ATTN_N_Q_HEADS, ATTN_HEAD_DIM), positions)
    k = rope(k.reshape(bsz, t_len, ATTN_N_KV_HEADS, ATTN_HEAD_DIM), positions)
    v = v.reshape(bsz, t_len, ATTN_N_KV_HEADS, ATTN_HEAD_DIM)
    y_a = sliding_window_attention(q, k, v, attn_sinks) @ w_attn_o
    merged = jax.nn.sigmoid(gate_s) * y_s + jax.nn.sigmoid(gate_a) * y_a
    return merged @ w_out

def setup_inputs(seed: int = 0) -> dict:
    key = jax.random.key(seed)
    ks = jax.random.split(key, 24)
    f32 = jnp.float32
    nl = DEPTH

    def nrm(k, shape, scale):
        return jax.random.normal(k, shape, f32) * scale

    x = nrm(ks[0], (BATCH, SEQ, D_MODEL), 1.0)
    positions = jnp.broadcast_to(jnp.arange(SEQ, dtype=jnp.int32), (BATCH, SEQ))
    ffn1_w_gate = nrm(ks[1], (nl, D_MODEL, FFN_HIDDEN), D_MODEL ** -0.5)
    ffn1_w_up = nrm(ks[2], (nl, D_MODEL, FFN_HIDDEN), D_MODEL ** -0.5)
    ffn1_w_down = nrm(ks[3], (nl, FFN_HIDDEN, D_MODEL), DEEPNORM_BETA * FFN_HIDDEN ** -0.5)
    ln1_g = 1.0 + nrm(ks[4], (nl, D_MODEL), 0.02)
    ln1_b = nrm(ks[5], (nl, D_MODEL), 0.02)
    w_in = nrm(ks[6], (nl, D_MODEL, PROJ_WIDTH), D_MODEL ** -0.5)
    conv_w = nrm(ks[7], (nl, SSD_CONV_WIDTH, SSD_XBC), SSD_CONV_WIDTH ** -0.5)
    conv_b = nrm(ks[8], (nl, SSD_XBC), 0.02)
    dt0 = jnp.exp(jax.random.uniform(ks[9], (nl, SSD_N_HEADS), f32, math.log(1e-3), math.log(1e-1)))
    dt_bias = dt0 + jnp.log(-jnp.expm1(-dt0))
    a_log = jnp.log(jax.random.uniform(ks[10], (nl, SSD_N_HEADS), f32, 1.0, 16.0))
    d_skip = 1.0 + nrm(ks[11], (nl, SSD_N_HEADS), 0.1)
    ssd_norm_g = 1.0 + nrm(ks[12], (nl, SSD_D_INNER), 0.02)
    w_ssd_o = nrm(ks[13], (nl, SSD_D_INNER, D_MODEL), SSD_D_INNER ** -0.5)
    attn_sinks = nrm(ks[14], (nl, ATTN_N_Q_HEADS), 0.5)
    w_attn_o = nrm(ks[15], (nl, ATTN_Q_WIDTH, D_MODEL), ATTN_Q_WIDTH ** -0.5)
    w_out = nrm(ks[16], (nl, D_MODEL, D_MODEL), DEEPNORM_BETA * D_MODEL ** -0.5)
    ln2_g = 1.0 + nrm(ks[17], (nl, D_MODEL), 0.02)
    ln2_b = nrm(ks[18], (nl, D_MODEL), 0.02)
    ffn2_w_gate = nrm(ks[19], (nl, D_MODEL, FFN_HIDDEN), D_MODEL ** -0.5)
    ffn2_w_up = nrm(ks[20], (nl, D_MODEL, FFN_HIDDEN), D_MODEL ** -0.5)
    ffn2_w_down = nrm(ks[21], (nl, FFN_HIDDEN, D_MODEL), DEEPNORM_BETA * FFN_HIDDEN ** -0.5)
    ln3_g = 1.0 + nrm(ks[22], (nl, D_MODEL), 0.02)
    ln3_b = nrm(ks[23], (nl, D_MODEL), 0.02)
    return {'x': x, 'positions': positions,
            'ffn1_w_gate': ffn1_w_gate, 'ffn1_w_up': ffn1_w_up, 'ffn1_w_down': ffn1_w_down,
            'ln1_g': ln1_g, 'ln1_b': ln1_b,
            'w_in': w_in, 'conv_w': conv_w, 'conv_b': conv_b, 'dt_bias': dt_bias, 'a_log': a_log,
            'd_skip': d_skip, 'ssd_norm_g': ssd_norm_g, 'w_ssd_o': w_ssd_o,
            'attn_sinks': attn_sinks, 'w_attn_o': w_attn_o, 'w_out': w_out,
            'ln2_g': ln2_g, 'ln2_b': ln2_b,
            'ffn2_w_gate': ffn2_w_gate, 'ffn2_w_up': ffn2_w_up, 'ffn2_w_down': ffn2_w_down,
            'ln3_g': ln3_g, 'ln3_b': ln3_b}

def reference(x, positions, ffn1_w_gate, ffn1_w_up, ffn1_w_down, ln1_g, ln1_b,
              w_in, conv_w, conv_b, dt_bias, a_log, d_skip, ssd_norm_g, w_ssd_o,
              attn_sinks, w_attn_o, w_out, ln2_g, ln2_b,
              ffn2_w_gate, ffn2_w_up, ffn2_w_down, ln3_g, ln3_b):
    h = x
    for l in range(DEPTH):
        h = layer_norm(DEEPNORM_ALPHA * h + 0.5 * swiglu(h, ffn1_w_gate[l], ffn1_w_up[l], ffn1_w_down[l]),
                       ln1_g[l], ln1_b[l])
        mix = hybrid_mixer(h, positions, w_in[l], conv_w[l], conv_b[l], dt_bias[l], a_log[l], d_skip[l],
                           ssd_norm_g[l], w_ssd_o[l], attn_sinks[l], w_attn_o[l], w_out[l])
        h = layer_norm(DEEPNORM_ALPHA * h + mix, ln2_g[l], ln2_b[l])
        h = layer_norm(DEEPNORM_ALPHA * h + 0.5 * swiglu(h, ffn2_w_gate[l], ffn2_w_up[l], ffn2_w_down[l]),
                       ln3_g[l], ln3_b[l])
    return h


_drawn_inputs = setup_inputs


def setup_inputs(seed=0):
    import zlib

    import numpy as np

    out = dict(_drawn_inputs(seed))
    spreads = {}
    factors = {'ln1_g': 2.694,
     'conv_b': 7.669,
     'd_skip': 25.312,
     'ssd_norm_g': 31.75,
     'attn_sinks': 45.728,
     'ln2_g': 2.799,
     'ln2_b': 2.808,
     'ln3_g': 8.01,
     'ln3_b': 8.155,
     'ln1_b': 4.093}
    for name, (base, spread) in spreads.items():
        noise = np.random.default_rng([zlib.crc32(name.encode()), seed]).standard_normal(out[name].shape)
        drawn = base * np.exp(spread * noise) if base else spread * noise
        out[name] = jnp.asarray(drawn.astype(out[name].dtype))
    for name, factor in factors.items():
        out[name] = (out[name] * factor).astype(out[name].dtype)
    return out
```

```python
from contextlib import ExitStack

import numpy as np

import concourse.bass as bass
from concourse import mybir

F32 = mybir.dt.float32
F32R = mybir.dt.float32r
I32 = mybir.dt.int32
ALU = mybir.AluOpType
ACT = mybir.ActivationFunctionType
AX = mybir.AxisListType

P = 128
SEQ = 256
TOK = SEQ // P
D = 2048
KD = D // P
F = 5632
KF = F // P
W = 512
NC_D = D // W
NC_F = F // W
DI = 4096
KI = DI // P
HEADS = 64
HD = 64
GROUPS = 8
HPG = HEADS // GROUPS
TPG = W // P
NS = 128
XBC = DI + 2 * GROUPS * NS
KX = XBC // P
CONV = 4
QH = 32
KVH = 4
QPK = QH // KVH
HALF = HD // 2
THETA = 10000.0
ALPHA = 2.0 ** 0.25
EPS = 1e-5
MASKED = -1e30

Z0 = 0
X0 = DI
B0 = X0 + DI
C0 = B0 + GROUPS * NS
DT0 = X0 + XBC
Q0 = DT0 + HEADS
K0 = Q0 + D
V0 = K0 + KVH * HD
GS0 = V0 + KVH * HD
GA0 = GS0 + D

SHARED_WAITS = (("ssd", 16), ("merge", 8))
LAND = 4
SPLIT = 4

PHASES = {
    "up1": (NC_F, [(8, 0), (8, 1)]),
    "down1": (2, [(22, 0), (22, 1)]),
    "kvdt": (1, [(8, 0), (8, 1)]),
    "attn": (KVH, [(8, 0), (8, 1)]),
    "attn_o": (2, [(8, 0), (8, 1)]),
    "ssd": (GROUPS // 2, [(8, 0), (8, 1), (8, 0), (8, 1), (8, 0), (8, 1)]),
    "merge": (NC_D, [(8, 0), (16, 1)]),
    "out": (1, [(8, 0), (8, 1), (8, 0), (8, 1)]),
    "up2": (NC_F, [(8, 0), (8, 1)]),
    "down2": (2, [(22, 0), (22, 1)]),
}
LN_USES = [(f"t{u}", u % 4) for u in range(8)]
SPARE = {
    "xT": (1, LN_USES),
    "up1": (NC_F, [("ga", 0), ("gb", 1)]),
    "ln1": (1, LN_USES),
    "prep": (1, [("ka", 0), ("kb", 1), ("acs", 2), ("rows", 3)]),
    "attn": (KVH, [("qa", 0), ("qb", 1)] + [(f"s{h}", h % 4) for h in range(QPK)]
             + [(f"p{h}", h % 4) for h in range(QPK)] + [("o0", 0), ("o1", 1), ("oa", 2), ("ob", 3)]),
    "ssd": (GROUPS, [("xa", 0), ("xb", 1), ("bc", 2), ("x0", 0), ("x1", 1), ("cb", 3),
                     ("st", 2), ("y0", 0), ("y1", 1), ("yoff", 3), ("ya", 2), ("yb", 3)]),
    "merge": (NC_D, [("ma", 0), ("mb", 1)]),
    "ln2": (1, LN_USES),
    "up2": (NC_F, [("ga", 0), ("gb", 1)]),
}
SPLIT_USES = {"xT": LN_USES, "up1": SPARE["up1"][1], "ln1": LN_USES, "attn": [("oa", 2), ("ob", 3)],
              "ssd": [("ya", 2), ("yb", 3)], "merge": SPARE["merge"][1], "ln2": LN_USES, "up2": SPARE["up2"][1]}
DEC_V = 4
DOWN_LINKS = {1: 4, 2: 6}
ATTN_LINKS = 8
SSD_LINKS = 2 * (3 + 3 * 2 * (CONV - 1))


def slab_bases():
    base, at = {}, 0
    for name, (n, chunks) in PHASES.items():
        per = sum(c[0] for c in chunks)
        base[name] = (at, per)
        at += n * per
    return base


SLABS = slab_bases()


def slab_no(phase, i, l):
    return SLABS[phase][0] + i * SLABS[phase][1] + l


def loads(phase, i, l):
    base, per = SLABS[phase]
    n = base // LAND + i * (per // LAND) + l // LAND + 1
    double = 8 // LAND
    if base > SLABS["ssd"][0]:
        n = n + GROUPS * double
    if phase == "ssd":
        n = n + i * (2 * double) + sum(m % 24 // 8 == 1 for m in range(l % LAND, l + 1, LAND))
    return n


def acc_use(phase, i, c):
    pair = PHASES[phase][1][c][1]
    at = 0
    for name, (n, chunks) in PHASES.items():
        per = sum(q == pair for _, q in chunks)
        if name == phase:
            return pair, at + i * per + sum(q == pair for _, q in chunks[:c])
        at += n * per


def spare_use(phase, u, what):
    names = [w for w, _ in SPARE[phase][1]]
    k = names.index(what)
    bank = SPARE[phase][1][k][1]
    at = 0
    for name, (n, uses) in SPARE.items():
        per = sum(b == bank for _, b in uses)
        if name == phase:
            return bank, at + u * per + sum(b == bank for _, b in uses[:k])
        at += n * per


def high_no(phase, u, what):
    at = 0
    for name, uses in SPLIT_USES.items():
        if name == phase:
            return at + u * len(uses) + [w for w, _ in uses].index(what)
        at += SPARE[name][0] * len(uses)


class Chain:

    def __init__(self, eng, sem):
        self.eng, self.sem, self.base, self.i, self.per, self.k = eng, sem, 0, 0, 0, 0

    def enter(self, i, first, per):
        self.base += self.k
        self.i, self.per, self.first, self.k = i, per, first, 0

    def leave(self, end):
        assert self.k == self.per, f"an iteration counts {self.k}"
        self.base, self.i, self.k = self.base + self.per * (end - self.first), 0, 0
        self.per = 0

    def now(self):
        if self.per:
            return self.base - self.first * self.per + self.k + self.i * self.per
        return self.base + self.k

    def link(self, ins):
        ins.then_inc(self.sem, 1)
        self.k += 1
        self.eng.wait_ge(self.sem, self.now())

    def mark(self, ins):
        ins.then_inc(self.sem, 1)
        self.k += 1
        return self.now()


def two_pi_parts():
    whole = 2 * np.pi
    a = np.floor(whole * 2.0 ** 9) / 2.0 ** 9
    b = np.floor((whole - a) * 2.0 ** 21) / 2.0 ** 21
    return float(a), float(b), float(np.float32(whole - a - b))


def build_decoder_layer(nc, x, positions, ffn1_w_gate, ffn1_w_up, ffn1_w_down, ln1_g, ln1_b, w_in, conv_w, conv_b,
                        dt_bias, a_log, d_skip, ssd_norm_g, w_ssd_o, attn_sinks, w_attn_o, w_out, ln2_g, ln2_b,
                        ffn2_w_gate, ffn2_w_up, ffn2_w_down, ln3_g, ln3_b, acs_rows, kept, out):
    ctx = ExitStack()

    def sb(name, shape, dt=F32):
        return ctx.enter_context(nc.sbuf_tensor(name, shape, dt))

    def sem(name):
        return ctx.enter_context(nc.semaphore(name))

    def tiles(w):
        return w[0].rearrange("(k p) n -> p k n", p=P)

    win, wso, wao, wou = tiles(w_in), tiles(w_ssd_o), tiles(w_attn_o), tiles(w_out)
    ffn_w = {1: (tiles(ffn1_w_gate), tiles(ffn1_w_up), tiles(ffn1_w_down)),
             2: (tiles(ffn2_w_gate), tiles(ffn2_w_up), tiles(ffn2_w_down))}
    x_view = x[0].rearrange("(t p) n -> p t n", p=P)
    kept_view = kept.rearrange("(t p) n -> p t n", p=P)
    out_view = out[0].rearrange("(t p) n -> p t n", p=P)

    with ctx:
        land = sb("land", [P, LAND, 2, W])
        w_hi = sb("w_hi", [P, SPLIT, 2, W], F32R)
        w_lo = sb("w_lo", [P, SPLIT, 2, W], F32R)
        resid = sb("resid", [P, TOK, D])
        gate_a = resid
        silu_t = resid[:, :, 0:W]
        prod = resid[:, :, W:2 * W]
        at0 = -(-nc.sbuf_base // 32) * 32
        sb("region", [P, 32 * 1024])

        def placed(name, shape, dt, at):
            return nc.alloc_sbuf_tensor_at(name, shape, dt, offset=at0 + at)

        K = 1024
        a_hi = placed("a_hi", [P, KD, SEQ], F32R, 96 * K)
        a_lo = placed("a_lo", [P, KD, SEQ], F32R, 112 * K)
        rows = placed("rows", [P, 2, D], F32, 96 * K)
        last_rows = placed("last_rows", [P, 2, D], F32, 112 * K)
        g_hi = placed("g_hi", [P, KF, SEQ], F32R, 0)
        g_lo = placed("g_lo", [P, KF, SEQ], F32R, 44 * K)
        y_hi = placed("y_hi", [P, KI, SEQ], F32R, 0)
        y_lo = placed("y_lo", [P, KI, SEQ], F32R, 32 * K)
        o_hi = placed("o_hi", [P, KD, SEQ], F32R, 64 * K)
        o_lo = placed("o_lo", [P, KD, SEQ], F32R, 80 * K)
        s_sb = placed("s_sb", [P, QPK, 3 * P], F32, 0)
        pT = placed("pT", [P, QPK, 3 * P], F32, 12 * K)
        qT = placed("qT", [P, TPG, SEQ], F32, 24 * K)
        q_rot = placed("q_rot", [P, TOK, W], F32, 28 * K)
        rot = placed("rot", [P, 4, W], F32, 32 * K)
        kT = placed("kT", [P, KVH, SEQ], F32, 40 * K)
        v_all = placed("v_all", [P, TOK, KVH * HD], F32, 44 * K)
        kT_j = placed("kT_j", [P, SEQ], F32, 46 * K)
        v_j = placed("v_j", [P, TOK, HD], F32, 47 * K)
        o_tok = placed("o_tok", [P, TOK, W], F32, 48 * K)
        k_rot = placed("k_rot", [P, TOK, KVH, 2, HD], F32, 52 * K)
        soft = placed("soft", [P, 64], F32, 56 * K)
        spl = placed("spl", [P, 6, TOK * HEADS], F32, 57 * K)
        rows_sb = placed("rows_sb", [HEADS, SEQ], F32, 60 * K)
        head_r = placed("head_r", [P, 3, HEADS], F32, 61 * K)
        seg = placed("seg", [P, 2, HPG, SEQ], F32, 64 * K)
        u_tok = placed("u_tok", [P, TOK, W], F32, 80 * K)
        conv = placed("conv", [P, TPG, SEQ], F32, 84 * K)
        t_tok = placed("t_tok", [P, TOK, W], F32, 84 * K)
        xs = placed("xs", [P, TOK, W], F32, 88 * K)
        x_end = placed("x_end", [P, W], F32, 92 * K)
        state = placed("state", [P, W], F32, 94 * K)
        sz = sb("sz", [P, TOK, W])
        bcT = sb("bcT", [P, 2, SEQ])
        b_tok = sb("b_tok", [P, P])
        cbm = sb("cbm", [P, TOK, P])
        ident = sb("ident", [P, P])
        upper = sb("upper", [P, P])
        ones = sb("ones", [P, P])
        mask = sb("mask", [P, 3 * P])
        vec_c = sb("vec_c", [P, GROUPS, 34])
        vec_d = sb("vec_d", [P, GROUPS, 7, HPG])
        grp_c = sb("grp_c", [P, 2, 34])
        grp_d = sb("grp_d", [P, 2, 7, HPG])
        ln_col = sb("ln_col", [P, 4, KD])
        sink_r = sb("sink_r", [P, QH])
        cosr = sb("cosr", [P, TOK, HALF])
        sinr = sb("sinr", [P, TOK, HALF])
        stats = sb("stats", [P, TOK, NC_D, 6])
        mv = sb("mv", [P, TOK, 2])
        rstd = sb("rstd", [P, TOK])
        shift = sb("shift", [P, TOK])
        rms = sb("rms", [P, TOK])
        eps = sb("eps", [P, 1])
        half_pi = sb("half_pi", [P, 1])
        par = placed("par", [P, 4, P], F32, 0)
        inv_f = placed("inv_f", [P, HALF], F32, 4 * K)
        pos_i = placed("pos_i", [P, TOK], I32, 5 * K)
        pos_f = placed("pos_f", [P, TOK], F32, 5 * K + 64)
        ang = placed("ang", [P, 6, TOK * HALF], F32, 6 * K)

        acc = ctx.enter_context(nc.psum_tensor("acc", [P, 4, W], F32))
        spare = ctx.enter_context(nc.psum_tensor("spare", [P, 4, W], F32))

        landed = [sem(f"landed{r}") for r in range(LAND)]
        high = sem("high")
        rest = sem("rest")
        used = sem("used")
        acc_out = [sem(f"acc_out{p}") for p in range(2)]
        bank_in = [sem(f"bank_in{b}") for b in range(4)]
        bank_out = [sem(f"bank_out{b}") for b in range(4)]
        tile_hi = sem("tile_hi")
        v_seq = sem("v_seq")
        s_seq = sem("s_seq")
        p_seq = sem("p_seq")
        x_in = sem("x_in")
        par_in = sem("par_in")
        row_in = sem("row_in")
        pos_in = sem("pos_in")
        setup = sem("setup")
        par_t = sem("par_t")
        trig = sem("trig")
        trig_s = sem("trig_s")
        dec_v = sem("dec_v")
        dec_s = sem("dec_s")
        v_kept = sem("v_kept")
        k_rotated = sem("k_rotated")
        rows_out = sem("rows_out")
        seg_in = [sem(f"seg_in{s}") for s in range(2)]
        args = sem("args")
        exps = sem("exps")
        mixed = sem("mixed")
        silu_x = sem("silu_x")
        silu_bc = sem("silu_bc")
        b_out = sem("b_out")
        gated = sem("gated")
        rms_s = sem("rms_s")
        scaled = sem("scaled")
        maxed = sem("maxed")
        prob = sem("prob")
        q_rotated = sem("q_rotated")
        kv_copy = sem("kv_copy")
        grp = sem("grp")
        ln_v = sem("ln_v")
        ln_s = sem("ln_s")
        ln_x = sem("ln_x")
        normed = sem("normed")
        rows_in = sem("rows_in")
        last_rows_in = sem("last_rows_in")
        resid_in = sem("resid_in")
        kept_out = sem("kept_out")
        stored = sem("stored")

        block = ctx.enter_context(nc.Block())

        @block.sync
        def _(sp):
            def load(phase, i, l, *sources, width=W):
                n = slab_no(phase, i, l)
                if not (phase == "up1" and isinstance(i, int) and n < LAND):
                    if (phase, l + 1) in SHARED_WAITS:
                        sp.wait_ge(rest, n - LAND + 2)
                    elif (phase, l) not in SHARED_WAITS:
                        sp.wait_ge(rest, n - LAND + 1)
                part = width // len(sources)
                for k, src in enumerate(sources):
                    sp.dma_start(land[:, l % LAND, :, k * part:(k + 1) * part], src).then_inc(landed[l % LAND], 16)

            def up(f, phase, i):
                for l in range(16):
                    k = 2 * (l % 8)
                    load(phase, i, l, ffn_w[f][l // 8][:, k:k + 2, bass.ds(i * W, W)])

            def down(f, phase):
                with sp.Fori(0, 2) as j:
                    for l in range(44):
                        c, k = l // 22, 2 * (l % 22)
                        load(phase, j, l, ffn_w[f][2][:, k:k + 2, bass.ds(j * 2 * W + c * W, W)])

            for c in range(NC_D):
                sp.dma_start(resid[:, :, c * W:(c + 1) * W], x_view[:, :, c * W:(c + 1) * W]).then_inc(x_in, 16)
            up(1, "up1", 0)
            with sp.Fori(1, NC_F) as i:
                up(1, "up1", i)
            down(1, "down1")
            for l in range(16):
                k = 2 * (l % 8)
                if l < 8:
                    load("kvdt", 0, l, win[:, k:k + 2, K0:K0 + W])
                else:
                    load("kvdt", 0, l, win[:, k:k + 2, DT0:DT0 + HEADS], width=HEADS)
            with sp.Fori(0, KVH) as j:
                for l in range(16):
                    k = 2 * (l % 8)
                    load("attn", j, l, win[:, k:k + 2, bass.ds(j * W + (Q0 if l < 8 else GA0), W)])
            with sp.Fori(0, 2) as j:
                for l in range(16):
                    k = 2 * (l % 8)
                    load("attn_o", j, l, wao[:, k:k + 2, bass.ds(j * 2 * W + (l // 8) * W, W)])
            with sp.Fori(0, GROUPS // 2) as i:
                for s in range(2):
                    for l in range(24):
                        k = 2 * (l % 8)
                        if l // 8 == 1:
                            load("ssd", i, s * 24 + l, *(win[:, k:k + 2, bass.ds(i * 2 * NS + (c + s * NS), NS)]
                                                         for c in (B0, C0)), width=2 * NS)
                        else:
                            c = (X0 if l < 8 else Z0) + s * W
                            load("ssd", i, s * 24 + l, win[:, k:k + 2, bass.ds(i * 2 * W + c, W)])
            with sp.Fori(0, NC_D) as i:
                for l in range(24):
                    if l < 8:
                        load("merge", i, l, win[:, 2 * l:2 * l + 2, bass.ds(i * W + GS0, W)])
                    else:
                        k = 2 * (l - 8)
                        load("merge", i, l, wso[:, k:k + 2, bass.ds(i * W, W)])
            for l in range(32):
                c, k = l // 8, 2 * (l % 8)
                load("out", 0, l, wou[:, k:k + 2, c * W:(c + 1) * W])
            with sp.Fori(0, NC_F) as i:
                up(2, "up2", i)
            down(2, "down2")
            sp.wait_ge(stored, 16 * NC_D)

        @block.gpsimd
        def _(pool):
            ch = Chain(pool, p_seq)
            ch.link(pool.memset(ident[:, :], 0.0))
            ch.link(pool.affine_select(out=ident[:, :], in_=ident[:, :], compare_op=ALU.not_equal, fill=1.0,
                                       base=0, pattern=[[-1, P]], channel_multiplier=1))
            pool.memset(eps[:, :], EPS)
            pool.memset(half_pi[:, :], float(np.pi / 2))
            inv_freq = (np.float32(THETA) ** (-np.arange(HALF, dtype=np.float32) * np.float32(2.0) / np.float32(HD)))
            for k in range(HALF):
                pool.memset(inv_f[:, k:k + 1], float(inv_freq[k]))
            pool.memset(ones[:, :], 1.0)
            pool.memset(upper[:, :], 1.0)
            ch.link(pool.memset(mask[:, :], 0.0))
            pool.affine_select(out=upper[:, :], in_=upper[:, :], compare_op=ALU.is_ge, fill=0.0,
                               base=0, pattern=[[1, P]], channel_multiplier=-1)
            for b in range(3):
                m = mask[:, b * P:(b + 1) * P]
                if b == 1:
                    last = pool.affine_select(out=m, in_=m, compare_op=ALU.is_gt, fill=MASKED,
                                              base=0, pattern=[[1, P]], channel_multiplier=-1)
                else:
                    last = pool.affine_select(out=m, in_=m, compare_op=ALU.is_ge, fill=MASKED,
                                              base=0, pattern=[[-1, P]], channel_multiplier=1)
            last.then_inc(setup, 1)
            def load_rows(dst, gain, bias, arrived):
                pool.dma_start(dst[:, 0, :], gain[0, :].partition_broadcast(P)).then_inc(arrived, 16)
                pool.dma_start(dst[:, 1, :], bias[0, :].partition_broadcast(P)).then_inc(arrived, 16)

            def hidden_complete(phase):
                bank, use = spare_use(phase, NC_F - 1, "gb")
                pool.wait_ge(bank_in[bank], use + 1)

            def keep_stream(first):
                for c in range(NC_D):
                    pool.wait_ge(ln_x, first + c + 1)
                    pool.dma_start(kept_view[:, :, c * W:(c + 1) * W], resid[:, :, c * W:(c + 1) * W]
                                   ).then_inc(kept_out, 16)

            hidden_complete("up1")
            pool.dma_start(resid[:, :, :], x_view).then_inc(resid_in, 16)
            keep_stream(0)
            with pool.Fori(0, KVH) as j:
                bank, use = spare_use("prep", 0, "kb")
                pool.wait_ge(bank_out[bank], use + 1)
                bank, use = spare_use("attn", j - 1, "s7")
                pool.wait_ge(bank_in[bank], use + 1)
                pool.tensor_copy(kT_j[:, :], kT[:, bass.ds(j, 1), :].rearrange("p a n -> p (a n)")).then_inc(kv_copy, 1)
                bank, use = spare_use("attn", j - 1, "o1")
                pool.wait_ge(bank_in[bank], use + 1)
                pool.tensor_copy(v_j[:, :, :], v_all[:, :, bass.ds(j * HD, HD)]).then_inc(kv_copy, 1)
            pool.wait_ge(dec_v, DEC_V)
            pool.wait_ge(rows_out, 16)
            pool.wait_ge(used, slab_no("attn_o", 1, 15) + 1)
            with pool.Fori(0, GROUPS // 2) as i:
                for s in range(2):
                    g = i * 2 + s
                    bank, use = spare_use("ssd", g - 2, "yb")
                    pool.wait_ge(bank_out[bank], use + 1)
                    pool.dma_start(seg[:, s, :, :], acs_rows[bass.ds(g * HPG, HPG), :].partition_broadcast(P)
                                   ).then_inc(seg_in[s], 16)
                    pool.tensor_copy(grp_c[:, s, :], vec_c[:, bass.ds(g, 1), :].rearrange("p a n -> p (a n)"))
                    pool.tensor_copy(grp_d[:, s, :, :], vec_d[:, bass.ds(g, 1), :, :].rearrange("p a b n -> p (a b) n")
                                     ).then_inc(grp, 1)
            pool.wait_ge(used, slab_no("merge", NC_D - 1, 7) + 1)
            load_rows(rows, ln1_g, ln1_b, rows_in)
            pool.wait_ge(gated, GROUPS + NC_D)
            pool.wait_ge(kept_out, 16 * NC_D)
            pool.dma_start(resid[:, :, :], kept_view).then_inc(resid_in, 16)
            keep_stream(NC_D)
            pool.wait_ge(used, slab_no("up2", NC_F - 1, 15) + 1)
            load_rows(rows, ln2_g, ln2_b, rows_in)
            hidden_complete("up2")
            pool.wait_ge(kept_out, 2 * 16 * NC_D)
            pool.dma_start(resid[:, :, :], kept_view).then_inc(resid_in, 16)
            load_rows(last_rows, ln3_g, ln3_b, last_rows_in)

        @block.tensor
        def _(pe):
            def free_bank(phase, u, what):
                bank, use = spare_use(phase, u, what)
                if not (isinstance(use, int) and use == 0):
                    pe.wait_ge(bank_out[bank], use)
                return bank

            def wait_bank(phase, u, what):
                bank, use = spare_use(phase, u, what)
                pe.wait_ge(bank_out[bank], use + 1)

            def turn(bank, at, src, rows=P):
                return pe.transpose(spare[0:src.shape[-1], bank, at:at + rows], src, ident[0:rows, 0:rows])

            def turn_rows(phase, u, names, src):
                for b, what in enumerate(names):
                    bank = free_bank(phase, u, what)
                    for k in range(2):
                        for t in range(TOK):
                            c = (2 * b + k) * P
                            last = turn(bank, k * SEQ + t * P, src[:, t, c:c + P])
                    last.then_inc(bank_in[bank], 1)

            def slab(phase, i, c, s, a, b, width=W):
                chunks = PHASES[phase][1]
                l = sum(n for n, _ in chunks[:c]) + s
                n_slabs = chunks[c][0]
                if s == 0:
                    pair, use = acc_use(phase, i, c)
                    if not (isinstance(use, int) and use == 0):
                        pe.wait_ge(acc_out[pair], use)
                pair = chunks[c][1]
                pe.wait_ge(rest, slab_no(phase, i, l) + 1)
                for k in range(2):
                    first, last = s == 0 and k == 0, s == n_slabs - 1 and k == 1
                    for t in range(TOK):
                        to = acc[:, 2 * pair + t, 0:width]
                        rows_hi = a[:, 2 * s + k, t * P:(t + 1) * P]
                        rows_lo = b[:, 2 * s + k, t * P:(t + 1) * P]
                        hi, lo = w_hi[:, l % SPLIT, k, 0:width], w_lo[:, l % SPLIT, k, 0:width]
                        pe.matmul(to, rows_hi, hi, start=first, stop=False)
                        pe.matmul(to, rows_hi, lo, start=False, stop=False)
                        mm = pe.matmul(to, rows_lo, hi, start=False, stop=last)
                mm.then_inc(used, 1)

            def ln_turn(phase, u, x_no):
                bank = free_bank(phase, 0, f"t{u}")
                if x_no is None:
                    if u == 0:
                        pe.wait_ge(x_in, 16 * NC_D)
                elif u % 2 == 0:
                    pe.wait_ge(ln_x, x_no + u // 2 + 1)
                for k in range(2):
                    for t in range(TOK):
                        c = (2 * u + k) * P
                        last = turn(bank, k * SEQ + t * P, resid[:, t, c:c + P])
                last.then_inc(bank_in[bank], 1)

            def up(phase, i, first, ln, x_no):
                for l in range(16):
                    if first and l < 8:
                        wait_bank(ln, 0, f"t{l}")
                    if phase == "up1" and first and l == 2:
                        pe.wait_ge(par_in, 16 * 8)
                        for q, rows in enumerate((2 * KX, 2 * KX, KX + KI, 4 * KD)):
                            last = pe.transpose(acc[:, 2, q * P:q * P + rows], par[0:rows, q, :], ident[0:rows, 0:rows])
                        last.then_inc(par_t, 1)
                    if phase == "up1" and first and l == 8:
                        pe.wait_ge(dec_v, 1)
                    if not first and l == 4:
                        up_turn(phase, i - 1)
                    slab(phase, i, l // 8, l % 8, a_hi, a_lo)
                    if first and l + 4 < 8:
                        ln_turn(ln, l + 4, x_no)

            def up_turn(phase, u):
                pair, use = acc_use(phase, u, 1)
                pe.wait_ge(acc_out[pair], use + 1)
                turn_rows(phase, u, ("ga", "gb"), prod)

            def ffn(f, ln, x_no):
                phase = f"up{f}"
                for u in range(4):
                    ln_turn(ln, u, x_no)
                up(phase, 0, True, ln, x_no)
                with pe.Fori(1, NC_F) as i:
                    up(phase, i, False, ln, x_no)
                up_turn(phase, NC_F - 1)
                wait_bank(phase, NC_F - 1, "ga")
                wait_bank(phase, NC_F - 1, "gb")
                with pe.Fori(0, 2) as j:
                    for l in range(44):
                        slab(f"down{f}", j, l // 22, l % 22, g_hi, g_lo)

            pe.wait_ge(p_seq, 2)
            ffn(1, "xT", None)

            for u in range(4):
                ln_turn("ln1", u, 0)
            for l in range(16):
                if l < 8:
                    wait_bank("ln1", 0, f"t{l}")
                slab("kvdt", 0, l // 8, l % 8, a_hi, a_lo, W if l < 8 else HEADS)
                if l + 4 < 8:
                    ln_turn("ln1", l + 4, 0)

            def scores(j, heads):
                if 0 in heads:
                    pe.wait_ge(kv_copy, 2 * j + 1)
                    wait_bank("attn", j, "qa")
                    wait_bank("attn", j, "qb")
                for h in heads:
                    bank = free_bank("attn", j, f"s{h}")
                    a = HD * (h % 2)
                    q, k = qT[a:a + HD, h // 2, :], kT_j[a:a + HD, :]
                    pe.matmul(spare[:, bank, 0:P], q[:, 0:P], k[:, 0:P], start=True, stop=True)
                    pe.matmul(spare[:, bank, P:3 * P], q[:, P:SEQ], k, start=True, stop=True
                              ).then_inc(bank_in[bank], 1)

            def turn_probs(j, heads):
                for h in heads:
                    pe.wait_ge(prob, j * QPK + h + 1)
                    bank = free_bank("attn", j, f"p{h}")
                    for b in range(3):
                        last = turn(bank, b * P, s_sb[:, h, b * P:(b + 1) * P])
                    last.then_inc(bank_in[bank], 1)

            def weighted(j):
                pe.wait_ge(kv_copy, 2 * j + 2)
                for h in range(QPK - 4, QPK):
                    wait_bank("attn", j, f"p{h}")
                bank = free_bank("attn", j, "o0")
                for h in range(QPK):
                    last = pe.matmul(spare[:, bank, h * HD:(h + 1) * HD], pT[:, h, 0:P], v_j[:, 0, :],
                                     start=True, stop=True)
                last.then_inc(bank_in[bank], 1)
                bank = free_bank("attn", j, "o1")
                for h in range(QPK):
                    to = spare[:, bank, h * HD:(h + 1) * HD]
                    pe.matmul(to, pT[:, h, P:2 * P], v_j[:, 0, :], start=True, stop=False)
                    last = pe.matmul(to, pT[:, h, 2 * P:3 * P], v_j[:, 1, :], start=False, stop=True)
                last.then_inc(bank_in[bank], 1)

            def attn_tail(j, at):
                if at == 0:
                    scores(j, (4, 5))
                if at == 1:
                    scores(j, (6, 7))
                if 5 <= at <= 8:
                    turn_probs(j, (2 * (at - 5), 2 * (at - 5) + 1))
                if at == 10:
                    weighted(j)
                if at == 13:
                    wait_bank("attn", j, "o0")
                    wait_bank("attn", j, "o1")
                    turn_rows("attn", j, ("oa", "ob"), o_tok)

            def attn(j, first):
                for l in range(16):
                    if first and l == 1:
                        pe.wait_ge(k_rotated, 1)
                        for b, what in enumerate(("ka", "kb")):
                            bank = free_bank("prep", 0, what)
                            for k in range(2):
                                for t in range(TOK):
                                    src = k_rot[:, t, 2 * b + k, :, :].rearrange("p a d -> p (a d)")
                                    last = turn(bank, k * SEQ + t * P, src)
                            last.then_inc(bank_in[bank], 1)
                    if first and l == 6:
                        decays_cumulated()
                    if not first:
                        attn_tail(j - 1, l)
                    if l == 12:
                        pe.wait_ge(q_rotated, j + 1)
                        turn_rows("attn", j, ("qa", "qb"), q_rot)
                    if l == 14:
                        scores(j, (0, 1))
                    if l == 15:
                        scores(j, (2, 3))
                    slab("attn", j, l // 8, l % 8, a_hi, a_lo)

            def decays_cumulated():
                pe.wait_ge(dec_v, 3)
                pe.wait_ge(setup, 1)
                adt = spl[:, 5, :].rearrange("p (t h) -> p t h", t=TOK)
                bank = free_bank("prep", 0, "acs")
                for t in range(TOK):
                    pe.matmul(spare[:, bank, t * HEADS:(t + 1) * HEADS], upper[:, :], adt[:, t, :], start=True, stop=True)
                pe.matmul(spare[:, bank, 2 * HEADS:3 * HEADS], ones[:, :], adt[:, 0, :], start=True, stop=True
                          ).then_inc(bank_in[bank], 1)
                bank = free_bank("prep", 0, "rows")
                for t in range(TOK):
                    last = pe.matmul(spare[0:HEADS, bank, t * P:(t + 1) * P], adt[:, t, :], upper[:, :],
                                     start=True, stop=True)
                last.then_inc(bank_in[bank], 1)

            attn(0, True)
            with pe.Fori(1, KVH) as j:
                attn(j, False)
            for at in range(16):
                attn_tail(KVH - 1, at)
            wait_bank("attn", KVH - 1, "oa")
            wait_bank("attn", KVH - 1, "ob")
            with pe.Fori(0, 2) as j:
                for l in range(16):
                    slab("attn_o", j, l // 8, l % 8, o_hi, o_lo)

            def ssd_tail(g, at):
                if at == 0:
                    pe.wait_ge(silu_bc, g + 1)
                    bank = free_bank("ssd", g, "cb")
                    turn(bank, 0, bcT[:, 0, 0:P])
                    for t in range(TOK):
                        last = pe.matmul(spare[:, bank, (1 + t) * P:(2 + t) * P], bcT[:, 0, t * P:(t + 1) * P],
                                         bcT[:, 1, t * P:(t + 1) * P], start=True, stop=True)
                    last.then_inc(bank_in[bank], 1)
                if at == 3:
                    pe.wait_ge(b_out, g + 1)
                    pe.wait_ge(mixed, 3 * g + 1)
                    bank = free_bank("ssd", g, "st")
                    pe.matmul(spare[:, bank, :], b_tok[:, :], x_end[:, :], start=True, stop=True
                              ).then_inc(bank_in[bank], 1)
                if at in (5, 6):
                    t = at - 5
                    pe.wait_ge(mixed, 3 * g + 2 + t)
                    bank = free_bank("ssd", g, f"y{t}")
                    for h in range(HPG):
                        last = pe.matmul(spare[:, bank, h * HD:(h + 1) * HD], seg_of(g)[:, h, t * P:(t + 1) * P],
                                         xs[:, t, h * HD:(h + 1) * HD], start=True, stop=True)
                    last.then_inc(bank_in[bank], 1)
                if at == 7:
                    wait_bank("ssd", g, "st")
                    bank = free_bank("ssd", g, "yoff")
                    pe.matmul(spare[:, bank, :], bcT[:, 1, P:SEQ], state[:, :], start=True, stop=True
                              ).then_inc(bank_in[bank], 1)
                if at == 14:
                    pe.wait_ge(scaled, g + 1)
                    turn_rows("ssd", g, ("ya", "yb"), sz)

            slot = [0]

            def seg_of(_):
                return seg[:, slot[0], :, :]

            def taken(i, c):
                pair, use = acc_use("ssd", i, c)
                pe.wait_ge(acc_out[pair], use + 1)

            def ssd(i, first):
                for s in range(2):
                    g = i * 2 + s
                    for l in range(24):
                        if not (first and s == 0):
                            slot[0] = 1 - s
                            ssd_tail(g - 1, l)
                        if l == 10:
                            taken(i, 3 * s)
                            turn_rows("ssd", g, ("xa", "xb"), u_tok)
                        if l == 19:
                            taken(i, 3 * s + 1)
                            bank = free_bank("ssd", g, "bc")
                            for k in range(2):
                                for t in range(TOK):
                                    last = turn(bank, k * SEQ + t * P, u_tok[:, t, k * P:(k + 1) * P])
                            last.then_inc(bank_in[bank], 1)
                        if l == 20:
                            pe.wait_ge(silu_x, g + 1)
                            for t in range(TOK):
                                bank = free_bank("ssd", g, f"x{t}")
                                for k in range(TPG):
                                    last = turn(bank, k * P, conv[:, k, t * P:(t + 1) * P])
                                last.then_inc(bank_in[bank], 1)
                        c = 3 * s + l // 8
                        slab("ssd", i, c, l % 8, a_hi, a_lo, 2 * NS if c % 3 == 1 else W)

            ssd(0, True)
            with pe.Fori(1, GROUPS // 2) as i:
                ssd(i, False)

            def merge_turn(u):
                pe.wait_ge(gated, GROUPS + u + 1)
                turn_rows("merge", u, ("ma", "mb"), sz)

            def merge(i, first):
                for l in range(24):
                    if first:
                        slot[0] = 1
                        ssd_tail(GROUPS - 1, l)
                        if l == 22:
                            wait_bank("ssd", GROUPS - 1, "ya")
                            wait_bank("ssd", GROUPS - 1, "yb")
                    elif l == 4:
                        merge_turn(i - 1)
                    if l < 8:
                        slab("merge", i, 0, l, a_hi, a_lo)
                    else:
                        slab("merge", i, 1, l - 8, y_hi, y_lo)

            merge(0, True)
            with pe.Fori(1, NC_D) as i:
                merge(i, False)
            for l in range(32):
                if l == 4:
                    merge_turn(NC_D - 1)
                if l == 6:
                    wait_bank("merge", NC_D - 1, "ma")
                    wait_bank("merge", NC_D - 1, "mb")
                if l == 0:
                    wait_bank("merge", NC_D - 2, "mb")
                slab("out", 0, l // 8, l % 8, o_hi, o_lo)
            ffn(2, "ln2", NC_D)

        @block.scalar
        def _(act):
            ch = Chain(act, s_seq)

            def split(phase, i, l, width=W):
                n = slab_no(phase, i, l)
                act.wait_ge(landed[l % LAND], loads(phase, i, l) * 16)
                if not (isinstance(n, int) and n < SPLIT):
                    act.wait_ge(used, n - SPLIT + 1)
                act.activation(w_hi[:, l % SPLIT, :, 0:width], land[:, l % LAND, :, 0:width], ACT.Copy
                               ).then_inc(high, 1)

            def bank_ready(phase, u, what):
                bank, use = spare_use(phase, u, what)
                act.wait_ge(bank_in[bank], use + 1)
                return bank

            def read_bank(phase, u, what):
                bank, use = spare_use(phase, u, what)
                act.wait_ge(bank_out[bank], use + 1)

            def acc_ready(phase, i, c):
                chunks = PHASES[phase][1]
                act.wait_ge(used, slab_no(phase, i, sum(n for n, _ in chunks[:c + 1]) - 1) + 1)
                pair = chunks[c][1]
                return pair, acc[:, 2 * pair:2 * pair + 2, :]

            def two_tiles(bank):
                return spare[:, bank, :].rearrange("p (k n) -> p k n", k=2)

            def high_tiles(phase, u, names, dst, k0, scale=1.0):
                for b, what in enumerate(names):
                    bank = bank_ready(phase, u, what)
                    act.activation(dst[:, bass.ds(k0 + 2 * b, 2), :], two_tiles(bank), ACT.Copy, scale=scale
                                   ).then_inc(tile_hi, 1)

            def ln_tile(phase, u, cols):
                bank = bank_ready(phase, 0, f"t{u}")
                if cols is None:
                    act.activation(a_hi[:, 2 * u:2 * u + 2, :], two_tiles(bank), ACT.Copy).then_inc(tile_hi, 1)
                    return
                for k in range(2):
                    last = act.activation(a_hi[:, 2 * u + k, :], two_tiles(bank)[:, k, :], ACT.Identity,
                                          scale=ln_col[:, cols, 2 * u + k:2 * u + k + 1],
                                          bias=ln_col[:, cols + 1, 2 * u + k:2 * u + k + 1])
                last.then_inc(tile_hi, 1)

            def root(no):
                act.wait_ge(ln_v, no)
                act.activation(rstd[:, :], mv[:, :, 1], ACT.Sqrt, bias=eps[:, :]).then_inc(ln_s, 1)

            def sines():
                act.wait_ge(setup, 1)
                act.wait_ge(trig, 1)
                ch.link(act.activation(ang[:, 5, :], ang[:, 4, :], ACT.Abs))
                flat = "p t n -> p (t n)"
                act.activation(sinr[:, :, :].rearrange(flat), ang[:, 4, :], ACT.Sin)
                act.activation(cosr[:, :, :].rearrange(flat), ang[:, 5, :], ACT.Sin, scale=-1.0, bias=half_pi[:, :]
                               ).then_inc(trig_s, 1)

            def up(phase, i, first, ln, cols):
                for l in range(16):
                    if first and l < 8:
                        ln_tile(ln, l, cols)
                    if phase == "up1" and first and l == 12:
                        sines()
                    if not first and l == 6:
                        high_tiles(phase, i - 1, ("ga", "gb"), g_hi, (i - 1) * 4)
                    if l == 10:
                        pair, gate = acc_ready(phase, i, 0)
                        _, use = acc_use(phase, i, 1)
                        if not (isinstance(use, int) and use == 0):
                            act.wait_ge(acc_out[1], use)
                        if phase == "up2" and first:
                            act.wait_ge(kept_out, 2 * 16 * NC_D)
                        act.activation(silu_t, gate, ACT.Silu).then_inc(acc_out[pair], 1)
                    split(phase, i, l)

            def ffn(f, ln, cols):
                phase = f"up{f}"
                up(phase, 0, True, ln, cols)
                with act.Fori(1, NC_F) as i:
                    up(phase, i, False, ln, cols)
                high_tiles(phase, NC_F - 1, ("ga", "gb"), g_hi, (NC_F - 1) * 4)
                with act.Fori(0, 2) as j:
                    for l in range(44):
                        split(f"down{f}", j, l)

            for src, q, r in ((conv_w[0, 0:2, :].rearrange("j (t p) -> (j t) p", p=P), 0, 0),
                              (conv_w[0, 2:4, :].rearrange("j (t p) -> (j t) p", p=P), 1, 0),
                              (conv_b[0].rearrange("(t p) -> t p", p=P), 2, 0),
                              (ssd_norm_g[0].rearrange("(t p) -> t p", p=P), 2, KX),
                              (ln1_g[0].rearrange("(t p) -> t p", p=P), 3, 0),
                              (ln1_b[0].rearrange("(t p) -> t p", p=P), 3, KD),
                              (ln2_g[0].rearrange("(t p) -> t p", p=P), 3, 2 * KD),
                              (ln2_b[0].rearrange("(t p) -> t p", p=P), 3, 3 * KD)):
                act.dma_start(par[r:r + src.shape[0], q, :], src).then_inc(par_in, 16)
            for t in range(TOK):
                act.dma_start(pos_i[:, t:t + 1], positions[0, t * P:(t + 1) * P].unsqueeze(1)).then_inc(pos_in, 16)
            act.dma_start(sink_r[:, :], attn_sinks[0].partition_broadcast(P)).then_inc(pos_in, 16)
            ffn(1, "xT", None)
            root(1)
            for k, src in enumerate((dt_bias, a_log, d_skip)):
                act.dma_start(head_r[:, k, :], src[0].partition_broadcast(P)).then_inc(row_in, 16)
            for l in range(16):
                if l < 8:
                    ln_tile("ln1", l, 0)
                if l == 11:
                    _, kv = acc_ready("kvdt", 0, 0)
                    act.activation(v_all[:, :, :], kv[:, :, KVH * HD:], ACT.Copy).then_inc(v_kept, 1)
                split("kvdt", 0, l, W if l < 8 else HEADS)

            def exp_head(j, h):
                act.wait_ge(maxed, 2 * j + h // 4 + 1)
                if h % 4 == 0:
                    act.activation(soft[:, 32 + 2 * h:40 + 2 * h], soft[:, 32 + 2 * h:40 + 2 * h], ACT.Exp)
                for b, (c0, c1) in enumerate(((0, P), (P, 3 * P))):
                    col = 2 * h + b
                    last = act.activation(s_sb[:, h, c0:c1], s_sb[:, h, c0:c1], ACT.Exp,
                                          bias=soft[:, 16 + col:17 + col], accum_out=soft[:, 48 + col:49 + col])
                last.then_inc(prob, 1)

            def attn_tail(j, at):
                if at == 2:
                    pair, gate = acc_ready("attn", j, 1)
                    act.activation(gate_a[:, :, bass.ds(j * W, W)], gate, ACT.Tanh, scale=0.5
                                   ).then_inc(acc_out[pair], 1)
                if 4 <= at <= 7:
                    exp_head(j, 2 * (at - 4))
                    exp_head(j, 2 * (at - 4) + 1)
                if at == 14:
                    high_tiles("attn", j, ("oa", "ob"), o_hi, j * 4)

            def attn(j, first):
                for l in range(16):
                    if not first:
                        attn_tail(j - 1, l)
                    if first and l == 1:
                        act.wait_ge(dec_v, 2)
                        act.wait_ge(row_in, 48)
                        act.activation(spl[:, 2, :], spl[:, 1, :], ACT.Exp)
                        act.activation(head_r[:, 1, :], head_r[:, 1, :], ACT.Exp).then_inc(dec_s, 1)
                    if first and l == 3:
                        for b, what in enumerate(("ka", "kb")):
                            bank = bank_ready("prep", 0, what)
                            act.activation(kT[:, 2 * b:2 * b + 2, :], two_tiles(bank), ACT.Copy
                                           ).then_inc(bank_out[bank], 1)
                    if first and l == 7:
                        bank = bank_ready("prep", 0, "rows")
                        act.activation(rows_sb[:, :], spare[0:HEADS, bank, 0:SEQ], ACT.Copy
                                       ).then_inc(bank_out[bank], 1)
                        _, use = spare_use("prep", 0, "rows")
                        act.wait_ge(bank_out[bank], use + 1)
                        act.dma_start(acs_rows, rows_sb[:, :]).then_inc(rows_out, 16)
                    if first and l == 8:
                        act.wait_ge(dec_v, 3)
                        _, use = spare_use("prep", 0, "acs")
                        act.wait_ge(bank_out[2], use + 1)
                        act.activation(spl[:, 0, 0:HEADS], spl[:, 0, 0:HEADS], ACT.Exp)
                        act.activation(vec_d[:, :, 5, :], vec_d[:, :, 1, :], ACT.Exp).then_inc(dec_s, 1)
                    if l == 13:
                        for b, what in enumerate(("qa", "qb")):
                            bank = bank_ready("attn", j, what)
                            act.activation(qT[:, 2 * b:2 * b + 2, :], two_tiles(bank), ACT.Copy
                                           ).then_inc(bank_out[bank], 1)
                    split("attn", j, l)

            attn(0, True)
            act.wait_ge(kept_out, 16 * NC_D)
            with act.Fori(1, KVH) as j:
                attn(j, False)
            for at in range(16):
                attn_tail(KVH - 1, at)
            with act.Fori(0, 2) as j:
                for l in range(16):
                    split("attn_o", j, l)

            def silu_z(i, c, g):
                pair, z = acc_ready("ssd", i, c)
                bank, use = spare_use("ssd", g - 1, "yb")
                act.wait_ge(bank_in[bank], use + 1)
                act.activation(sz[:, :, :], z, ACT.Silu).then_inc(acc_out[pair], 1)

            def ssd_tail(i, s, g, at):
                if at == 1:
                    bank = bank_ready("ssd", g, "cb")
                    act.activation(b_tok[:, :], spare[:, bank, 0:P], ACT.Copy).then_inc(b_out, 1)
                if at == 3:
                    silu_z(i, 3 * s + 2, g)
                if at == 5:
                    bank = bank_ready("ssd", g, "st")
                    act.activation(state[:, :], spare[:, bank, :], ACT.Copy).then_inc(bank_out[bank], 1)
                if at == 12:
                    act.wait_ge(gated, g + 1)
                    for t in range(TOK):
                        last = act.activation(t_tok[:, t, :], sz[:, t, :], ACT.Square, accum_out=rms[:, t:t + 1])
                    ch.link(last)
                    act.activation(rms[:, :], rms[:, :], ACT.Sqrt, scale=1.0 / W, bias=eps[:, :]).then_inc(rms_s, 1)
                if at == 16:
                    for b, what in enumerate(("ya", "yb")):
                        bank = bank_ready("ssd", g, what)
                        for k in range(2):
                            ct = 2 * b + k
                            last = act.activation(y_hi[:, bass.ds(g * TPG + ct, 1), :], two_tiles(bank)[:, k:k + 1, :],
                                                  ACT.Copy, scale=grp_c[:, s, 30 + ct:31 + ct])
                        last.then_inc(tile_hi, 1)

            def ssd(i, first):
                for s in range(2):
                    g = i * 2 + s
                    for l in range(24):
                        if not (first and s == 0):
                            ssd_tail(i - 1 + s, 1 - s, g - 1, l)
                        if l in (6, 7):
                            t = l - 6
                            act.wait_ge(args, 2 * g + t + 1)
                            view = seg[:, s, :, t * P:(t + 1) * P]
                            act.activation(view, view, ACT.Exp).then_inc(exps, 1)
                        if l == 9:
                            pair, x_acc = acc_ready("ssd", i, 3 * s)
                            if not (first and s == 0):
                                bank_ready("ssd", g - 1, "bc")
                            act.activation(u_tok[:, :, :], x_acc, ACT.Copy).then_inc(acc_out[pair], 1)
                        if l == 18:
                            pair, bc = acc_ready("ssd", i, 3 * s + 1)
                            bank_ready("ssd", g, "xb")
                            act.activation(u_tok[:, :, 0:2 * NS], bc[:, :, 0:2 * NS], ACT.Copy
                                           ).then_inc(acc_out[pair], 1)
                        if l == 19:
                            read_bank("ssd", g, "xa")
                            read_bank("ssd", g, "xb")
                            act.activation(conv[:, :, :], conv[:, :, :], ACT.Silu).then_inc(silu_x, 1)
                        if l == 22:
                            for t in range(TOK):
                                bank = bank_ready("ssd", g, f"x{t}")
                                act.activation(xs[:, t, :], spare[:, bank, :], ACT.Copy).then_inc(bank_out[bank], 1)
                        if l == 23:
                            read_bank("ssd", g, "bc")
                            act.activation(bcT[:, :, :], bcT[:, :, :], ACT.Silu).then_inc(silu_bc, 1)
                        split("ssd", i, s * 24 + l, W if l // 8 != 1 else 2 * NS)

            ssd(0, True)
            with act.Fori(1, GROUPS // 2) as i:
                ch.enter(i, 1, 2)
                ssd(i, False)
                ch.leave(GROUPS // 2)

            def merge_high(u):
                high_tiles("merge", u, ("ma", "mb"), o_hi, u * 4, 0.5)

            def merge(i, first):
                for l in range(24):
                    if first:
                        ssd_tail(GROUPS // 2 - 1, 1, GROUPS - 1, l)
                    elif l == 6:
                        merge_high(i - 1)
                    if l == 17:
                        pair, gate = acc_ready("merge", i, 0)
                        if first:
                            bank_ready("ssd", GROUPS - 1, "yb")
                        else:
                            bank_ready("merge", i - 1, "mb")
                        act.activation(sz[:, :, :], gate, ACT.Tanh, scale=0.5).then_inc(acc_out[pair], 1)
                    split("merge", i, l)

            merge(0, True)
            with act.Fori(1, NC_D) as i:
                merge(i, False)
            for l in range(32):
                if l == 5:
                    merge_high(NC_D - 1)
                split("out", 0, l)
            root(2)
            ffn(2, "ln2", 2)
            root(3)
            act.wait_ge(ln_x, 2 * NC_D + 1)
            for c in range(NC_D):
                for t in range(TOK):
                    part = resid[:, t, c * W:(c + 1) * W]
                    last = act.activation(part, part, ACT.Identity, scale=rstd[:, t:t + 1], bias=shift[:, t:t + 1])
                last.then_inc(normed, 1)
            for c in range(NC_D):
                act.wait_ge(ln_x, 2 * NC_D + 2 + c)
                act.dma_start(out_view[:, :, c * W:(c + 1) * W], resid[:, :, c * W:(c + 1) * W]).then_inc(stored, 16)

        @block.vector
        def _(dve):
            ch = Chain(dve, v_seq)

            def split(phase, i, l, width=W):
                dve.wait_ge(high, slab_no(phase, i, l) + 1)
                dve.tensor_tensor(w_lo[:, l % SPLIT, :, 0:width], land[:, l % LAND, :, 0:width],
                                  w_hi[:, l % SPLIT, :, 0:width].bitcast(F32), ALU.subtract).then_inc(rest, 1)

            def bank_ready(phase, u, what):
                bank, use = spare_use(phase, u, what)
                dve.wait_ge(bank_in[bank], use + 1)
                return bank

            def read_done(phase, u, what):
                bank, use = spare_use(phase, u, what)
                dve.wait_ge(bank_out[bank], use + 1)

            def acc_ready(phase, i, c):
                chunks = PHASES[phase][1]
                dve.wait_ge(used, slab_no(phase, i, sum(n for n, _ in chunks[:c + 1]) - 1) + 1)
                pair = chunks[c][1]
                return pair, acc[:, 2 * pair:2 * pair + 2, :]

            def two_tiles(bank):
                return spare[:, bank, :].rearrange("p (k n) -> p k n", k=2)

            def rest_tiles(phase, u, names, hi, lo, k0, scale=1.0):
                for b, what in enumerate(names):
                    bank = bank_ready(phase, u, what)
                    dve.wait_ge(tile_hi, high_no(phase, u, what) + 1)
                    at = bass.ds(k0 + 2 * b, 2)
                    dve.scalar_tensor_tensor(out=lo[:, at, :], in0=two_tiles(bank), scalar=scale,
                                             in1=hi[:, at, :].bitcast(F32), op0=ALU.mult, op1=ALU.subtract
                                             ).then_inc(bank_out[bank], 1)

            def ln_tile(phase, u, cols):
                what = f"t{u}"
                bank = bank_ready(phase, 0, what)
                at = slice(2 * u, 2 * u + 2)
                dve.wait_ge(tile_hi, high_no(phase, 0, what) + 1)
                if cols is None:
                    dve.tensor_tensor(a_lo[:, at, :], two_tiles(bank), a_hi[:, at, :].bitcast(F32), ALU.subtract
                                      ).then_inc(bank_out[bank], 1)
                    return
                h = sz[:, u % 2, :].rearrange("p (k n) -> p k n", k=2)
                for k in range(2):
                    last = dve.tensor_scalar(h[:, k, :], two_tiles(bank)[:, k, :],
                                             ln_col[:, cols, 2 * u + k:2 * u + k + 1],
                                             ln_col[:, cols + 1, 2 * u + k:2 * u + k + 1], ALU.mult, ALU.add)
                ch.link(last)
                dve.tensor_tensor(a_lo[:, at, :], h, a_hi[:, at, :].bitcast(F32), ALU.subtract
                                  ).then_inc(bank_out[bank], 1)

            def statistics(c):
                for t in range(TOK):
                    last = dve.bn_stats(stats[:, t, c, :] if isinstance(c, int) else
                                        stats[:, t, bass.ds(c, 1), :].rearrange("p a n -> p (a n)"),
                                        resid[:, t, bass.ds(c * W, W)])
                return last

            def evacuate(phase, i, cc, c, scale):
                pair, product = acc_ready(phase, i, cc)
                part = resid[:, :, bass.ds(c * W, W)]
                dve.scalar_tensor_tensor(out=part, in0=product, scalar=scale, in1=part, op0=ALU.mult, op1=ALU.add
                                         ).then_inc(acc_out[pair], 1)
                _, use = acc_use(phase, i, cc)
                dve.wait_ge(acc_out[pair], use + 1)
                ch.link(statistics(c))

            def prepare_rows(fills, c):
                part = resid[:, :, bass.ds(c * W, W)]
                dve.wait_ge(resid_in, (fills + 1) * 16)
                dve.wait_ge(rows_in, fills * 32)
                gain, bias = (rows[:, k:k + 1, bass.ds(c * W, W)].to_broadcast([P, TOK, W]) for k in range(2))
                ch.link(dve.scalar_tensor_tensor(out=part, in0=part, scalar=ALPHA, in1=gain, op0=ALU.mult,
                                                 op1=ALU.mult))
                ch.link(dve.scalar_tensor_tensor(out=part, in0=bias, scalar=ALPHA, in1=part, op0=ALU.mult,
                                                 op1=ALU.add))

            def normalise(no, chunks=True):
                for t in range(TOK):
                    last = dve.bn_aggr(mv[:, t, :], stats[:, t, :, :].rearrange("p c n -> p (c n)"))
                last.then_inc(ln_v, 1)
                dve.wait_ge(ln_s, no)
                ch.link(dve.reciprocal(rstd[:, :], rstd[:, :]))

            def ln_chunk(c):
                for t in range(TOK):
                    part = resid[:, t, c * W:(c + 1) * W]
                    last = dve.tensor_scalar(part, part, mv[:, t, 0:1], rstd[:, t:t + 1], ALU.subtract, ALU.mult)
                last.then_inc(ln_x, 1)

            def product(phase, i):
                pair, use = acc_use(phase, i, 0)
                dve.wait_ge(acc_out[pair], use + 1)
                pair, upper_half = acc_ready(phase, i, 1)
                if not (isinstance(i, int) and i == 0):
                    bank_ready(phase, i - 1, "gb")
                dve.tensor_tensor(prod, silu_t, upper_half, ALU.mult).then_inc(acc_out[pair], 1)

            def up(phase, i, first, ln, cols):
                for l in range(16):
                    if first and l < 8:
                        ln_tile(ln, l, cols)
                        if cols is not None and l in (0, 1):
                            ln_chunk(l + 2)
                    if not first and l == 2:
                        product_of(phase, i)
                    if not first and l == 7:
                        rest_tiles(phase, i - 1, ("ga", "gb"), g_hi, g_lo, (i - 1) * 4)
                    if phase == "up1" and first and l == 4:
                        columns()
                    if phase == "up1" and first and l == 9:
                        angles()
                    split(phase, i, l)

            def product_of(phase, i):
                product(phase, i - 1)

            def down(f, j, loop_c):
                phase = f"down{f}"
                for l in range(44):
                    if l in (4, 26):
                        cc = l // 22
                        c = loop_c + cc
                        if f == 1:
                            part = resid[:, :, bass.ds(c * W, W)]
                            dve.wait_ge(resid_in, 16)
                            ch.link(dve.tensor_scalar(part, part, ALPHA, None, ALU.mult))
                        else:
                            prepare_rows(2, c)
                    if l == 24:
                        evacuate(phase, j, 0, loop_c, 0.5)
                    split(phase, j, l)
                evacuate(phase, j, 1, loop_c + 1, 0.5)

            def ffn(f, ln, cols):
                phase = f"up{f}"
                up(phase, 0, True, ln, cols)
                with dve.Fori(1, NC_F) as i:
                    up(phase, i, False, ln, cols)
                product(phase, NC_F - 1)
                rest_tiles(phase, NC_F - 1, ("ga", "gb"), g_hi, g_lo, (NC_F - 1) * 4)
                with dve.Fori(0, 2) as j:
                    ch.enter(j, 0, DOWN_LINKS[f])
                    down(f, j, j * 2)
                    ch.leave(2)

            def columns():
                dve.wait_ge(par_t, 1)
                col = acc[:, 2, :]
                for j in range(CONV + 1):
                    at = [0, KX, P, P + KX, 2 * P][j]
                    dve.tensor_copy(vec_c[:, :, 0:20].rearrange("p g (c j) -> p g c j", j=5)[:, :, :, j],
                                    col[:, at:at + KI].rearrange("p (g c) -> p g c", c=TPG))
                    dve.tensor_copy(vec_c[:, :, 20:30].rearrange("p g (c j) -> p g c j", j=5)[:, :, :, j],
                                    col[:, at + KI:at + KX].rearrange("p (c g) -> p g c", c=2))
                dve.tensor_copy(vec_c[:, :, 30:34], col[:, 2 * P + KX:2 * P + KX + KI].rearrange("p (g c) -> p g c", c=TPG))
                dve.tensor_copy(ln_col[:, :, :], col[:, 3 * P:3 * P + 4 * KD].rearrange("p (a k) -> p a k", a=4)
                                ).then_inc(dec_v, 1)

            def angles():
                a, b, c = two_pi_parts()
                magic = 1.5 * 2.0 ** 23
                big = 1024.0
                dve.wait_ge(pos_in, 16 * (TOK + 1))
                dve.wait_ge(setup, 1)
                ch.link(dve.tensor_copy(pos_f[:, :], pos_i[:, :]))
                angle, n, hi, lo, r = (ang[:, k, :] for k in range(5))
                ch.link(dve.tensor_tensor(angle.rearrange("p (t n) -> p t n", t=TOK),
                                          pos_f[:, :].unsqueeze(2).to_broadcast([P, TOK, HALF]),
                                          inv_f[:, :].unsqueeze(1).to_broadcast([P, TOK, HALF]), ALU.mult))

                def whole(src, scale):
                    ch.link(dve.tensor_scalar(n, src, scale, magic, ALU.mult, ALU.add))
                    ch.link(dve.tensor_scalar(n, n, magic, None, ALU.subtract))

                def less(dst, src, part):
                    ch.link(dve.scalar_tensor_tensor(out=dst, in0=n, scalar=-part, in1=src, op0=ALU.mult, op1=ALU.add))

                whole(angle, float(1.0 / (2 * np.pi * big)))
                less(hi, angle, a * big)
                less(hi, hi, b * big)
                ch.link(dve.tensor_scalar(lo, n, -c * big, None, ALU.mult))
                whole(hi, float(1.0 / (2 * np.pi)))
                less(hi, hi, a)
                less(hi, hi, b)
                ch.link(dve.tensor_tensor(hi, hi, lo, ALU.add))
                less(r, hi, c)
                pi = float(np.nextafter(np.float32(np.pi), np.float32(0)))
                dve.tensor_scalar(r, r, pi, -pi, ALU.min, ALU.max).then_inc(trig, 1)

            ffn(1, "xT", None)

            def rotate(src, dst_lo, dst_hi, heads, signal):
                shape = [P, TOK, heads, HALF]
                cos = cosr[:, :, :].unsqueeze(2).to_broadcast(shape)
                sin = sinr[:, :, :].unsqueeze(2).to_broadcast(shape)
                u1, u2 = src[:, :, :, 0:HALF], src[:, :, :, HALF:HD]
                n = TOK * heads * HALF
                tmp = [rot[:, k, 0:n].rearrange("p (t h d) -> p t h d", t=TOK, h=heads) for k in range(4)]
                dve.tensor_tensor(tmp[0], u1, cos, ALU.mult)
                dve.tensor_tensor(tmp[1], u2, sin, ALU.mult)
                dve.tensor_tensor(tmp[2], u2, cos, ALU.mult)
                signal(dve.tensor_tensor(tmp[3], u1, sin, ALU.mult))
                for d in dst_lo:
                    dve.tensor_tensor(d, tmp[0], tmp[1], ALU.subtract)
                for d in dst_hi:
                    last = dve.tensor_tensor(d, tmp[2], tmp[3], ALU.add)
                return last

            normalise(1)
            ln_chunk(0)
            ln_chunk(1)
            for l in range(16):
                if l < 8:
                    ln_tile("ln1", l, 0)
                    if l in (0, 1):
                        ln_chunk(l + 2)
                if l == 13:
                    pair, kv = acc_ready("kvdt", 0, 0)
                    dve.wait_ge(trig_s, 1)
                    dve.wait_ge(v_kept, 1)

                    def free_kv(ins):
                        ins.then_inc(acc_out[0], 1)
                        dve.wait_ge(acc_out[0], acc_use("kvdt", 0, 0)[1] + 1)

                    rotate(kv[:, :, 0:KVH * HD].rearrange("p t (h d) -> p t h d", d=HD),
                           [k_rot[:, :, :, d, 0:HALF] for d in range(2)],
                           [k_rot[:, :, :, d, HALF:HD] for d in range(2)], KVH, free_kv).then_inc(k_rotated, 1)
                split("kvdt", 0, l, W if l < 8 else HEADS)

            def time_steps(part):
                v, neg, e, s, dt, adt = (spl[:, k, :] for k in range(6))
                by_token = "p (t h) -> p t h"

                def row(k):
                    return head_r[:, k:k + 1, :].to_broadcast([P, TOK, HEADS])

                if part == 0:
                    pair, raw = acc_ready("kvdt", 0, 1)
                    dve.wait_ge(row_in, 48)
                    dve.tensor_tensor(v.rearrange(by_token, t=TOK), raw[:, :, 0:HEADS], row(0), ALU.add
                                      ).then_inc(acc_out[pair], 1)
                    dve.wait_ge(acc_out[pair], acc_use("kvdt", 0, 1)[1] + 1)
                    dve.scalar_tensor_tensor(out=neg, in0=v, scalar=-1.0, in1=v, op0=ALU.mult, op1=ALU.min
                                             ).then_inc(dec_v, 1)
                if part == 1:
                    dve.wait_ge(dec_s, 1)
                    ch.link(dve.tensor_scalar(s, e, 2.0, None, ALU.add))
                    ch.link(dve.reciprocal(s, s))
                    ch.link(dve.tensor_tensor(s, e, s, ALU.mult))
                    q, r = neg, e
                    ch.link(dve.tensor_tensor(q, s, s, ALU.mult))
                    ch.link(dve.tensor_scalar(r, q, 1.0 / 17, None, ALU.mult))
                    for k in range(7, 3, -1):
                        ch.link(dve.scalar_tensor_tensor(out=r, in0=r, scalar=1.0 / (2 * k + 1), in1=q,
                                                         op0=ALU.add, op1=ALU.mult))
                if part == 2:
                    q, r = neg, e
                    for k in range(3, 0, -1):
                        ch.link(dve.scalar_tensor_tensor(out=r, in0=r, scalar=1.0 / (2 * k + 1), in1=q,
                                                         op0=ALU.add, op1=ALU.mult))
                    ch.link(dve.scalar_tensor_tensor(out=r, in0=r, scalar=1.0, in1=s, op0=ALU.add, op1=ALU.mult))
                    ch.link(dve.tensor_scalar(v, v, 0.0, None, ALU.max))
                    ch.link(dve.scalar_tensor_tensor(out=dt, in0=r, scalar=2.0, in1=v, op0=ALU.mult, op1=ALU.add))
                    dve.scalar_tensor_tensor(out=adt.rearrange(by_token, t=TOK), in0=dt.rearrange(by_token, t=TOK),
                                             scalar=-1.0, in1=row(1), op0=ALU.mult, op1=ALU.mult).then_inc(dec_v, 1)
                by_group = "p (g h) -> p g h"
                if part == 3:
                    bank = bank_ready("prep", 0, "acs")
                    for t in range(TOK):
                        last = dve.tensor_copy(vec_d[:, :, t, :],
                                               spare[:, bank, t * HEADS:(t + 1) * HEADS].rearrange(by_group, h=HPG))
                        dve.tensor_copy(vec_d[:, :, 2 + t, :], dt[:, t * HEADS:(t + 1) * HEADS].rearrange(by_group, h=HPG))
                    ch.link(dve.tensor_copy(vec_d[:, :, 6, :], head_r[:, 2, :].rearrange(by_group, h=HPG)))
                    dve.tensor_tensor(v[:, 0:HEADS].rearrange(by_group, h=HPG),
                                      spare[:, bank, 2 * HEADS:3 * HEADS].rearrange(by_group, h=HPG),
                                      vec_d[:, :, 0, :], ALU.subtract).then_inc(bank_out[bank], 1)
                if part == 4:
                    dve.wait_ge(dec_s, 2)
                    dve.tensor_tensor(vec_d[:, :, 4, :], v[:, 0:HEADS].rearrange(by_group, h=HPG), vec_d[:, :, 2, :],
                                      ALU.mult).then_inc(dec_v, 1)

            def score(j, heads):
                for h in heads:
                    bank = bank_ready("attn", j, f"s{h}")
                    dve.scalar_tensor_tensor(out=s_sb[:, h, :], in0=spare[:, bank, 0:3 * P], scalar=HD ** -0.5,
                                             in1=mask[:, :], op0=ALU.mult, op1=ALU.add).then_inc(bank_out[bank], 1)

            def maxima(j, half):
                for h in range(4 * half, 4 * half + 4):
                    read_done("attn", j, f"s{h}")
                h0 = 4 * half
                mx = soft[:, 2 * h0:2 * h0 + 8].rearrange("p (h b) -> p h b", b=2)
                dve.tensor_reduce(mx[:, :, 0], s_sb[:, h0:h0 + 4, 0:P], AX.X, ALU.max)
                ch.link(dve.tensor_reduce(mx[:, :, 1], s_sb[:, h0:h0 + 4, P:3 * P], AX.X, ALU.max))
                sink = sink_r[:, bass.ds(j * QPK + h0, 4)].unsqueeze(2).to_broadcast([P, 4, 2])
                ch.link(dve.tensor_tensor(mx, mx, sink, ALU.max))
                neg = soft[:, 16 + 2 * h0:24 + 2 * h0]
                ch.link(dve.tensor_scalar(neg, soft[:, 2 * h0:2 * h0 + 8], -1.0, None, ALU.mult))
                dve.tensor_tensor(soft[:, 32 + 2 * h0:40 + 2 * h0].rearrange("p (h b) -> p h b", b=2), sink,
                                  neg.rearrange("p (h b) -> p h b", b=2), ALU.add).then_inc(maxed, 1)

            def attn_tail(j, at):
                if at < 3:
                    score(j, (2 * at + 2, 2 * at + 3))
                if at in (3, 4):
                    maxima(j, at - 3)
                if 6 <= at <= 9:
                    for h in (2 * (at - 6), 2 * (at - 6) + 1):
                        bank = bank_ready("attn", j, f"p{h}")
                        dve.tensor_copy(pT[:, h, :], spare[:, bank, 0:3 * P]).then_inc(bank_out[bank], 1)
                if at == 11:
                    dve.wait_ge(prob, j * QPK + QPK)
                    den = soft[:, 48:64]
                    ch.link(dve.tensor_tensor(den, den, soft[:, 32:48], ALU.add))
                    ch.link(dve.reciprocal(den, den))
                    for t in range(TOK):
                        bank = bank_ready("attn", j, f"o{t}")
                        dve.tensor_tensor(o_tok[:, t, :].rearrange("p (h d) -> p h d", d=HD),
                                          spare[:, bank, :].rearrange("p (h d) -> p h d", d=HD),
                                          den.rearrange("p (h b) -> p h b", b=2)[:, :, t:t + 1].to_broadcast([P, QPK, HD]),
                                          ALU.mult).then_inc(bank_out[bank], 1)
                if at == 15:
                    rest_tiles("attn", j, ("oa", "ob"), o_hi, o_lo, j * 4)

            def attn(j, first):
                for l in range(16):
                    if first and l < 3:
                        time_steps(l)
                    if first and l == 7:
                        time_steps(3)
                    if first and l == 9:
                        time_steps(4)
                    if not first:
                        attn_tail(j - 1, l)
                    if l == 10:
                        pair, q = acc_ready("attn", j, 0)
                        _, use = acc_use("attn", j, 0)

                        def free_q(ins):
                            ins.then_inc(acc_out[0], 1)
                            dve.wait_ge(acc_out[0], use + 1)

                        view = q_rot[:, :, :].rearrange("p t (h d) -> p t h d", d=HD)
                        rotate(q.rearrange("p t (h d) -> p t h d", d=HD), [view[:, :, :, 0:HALF]],
                               [view[:, :, :, HALF:HD]], QPK, free_q).then_inc(q_rotated, 1)
                    if l == 15:
                        score(j, (0, 1))
                    split("attn", j, l)

            attn(0, True)
            with dve.Fori(1, KVH) as j:
                ch.enter(j, 1, ATTN_LINKS)
                attn(j, False)
                ch.leave(KVH)
            for at in range(16):
                attn_tail(KVH - 1, at)

            def gate_attention(j, cc):
                pair, y_a = acc_ready("attn_o", j, cc)
                part = gate_a[:, :, bass.ds((j * 2 + cc) * W, W)]
                dve.scalar_tensor_tensor(out=part, in0=part, scalar=1.0, in1=y_a, op0=ALU.add, op1=ALU.mult
                                         ).then_inc(acc_out[pair], 1)

            dve.wait_ge(acc_out[1], acc_use("attn", KVH - 1, 1)[1] + 1)
            with dve.Fori(0, 2) as j:
                for l in range(16):
                    if l == 10:
                        gate_attention(j, 0)
                    split("attn_o", j, l)
                gate_attention(j, 1)

            def heads_of(view, n=W):
                return view.rearrange("p (h d) -> p h d", d=HD)

            def ssd_tail(i, s, g, at):
                col = grp_d[:, s, :, :]
                if at == 1:
                    bank = bank_ready("ssd", g, "cb")
                    dve.wait_ge(b_out, g + 1)
                    dve.tensor_tensor(cbm[:, :, :], spare[:, bank, P:3 * P].rearrange("p (t n) -> p t n", t=TOK),
                                      upper[:, :].unsqueeze(1).to_broadcast([P, TOK, P]), ALU.mult
                                      ).then_inc(bank_out[bank], 1)
                    for t in range(TOK):
                        bank, use = spare_use("ssd", g, f"x{t}")
                        dve.wait_ge(bank_out[bank], use + 1)
                    dve.tensor_tensor(heads_of(x_end[:, :]), heads_of(xs[:, 0, :]),
                                      col[:, 4, :].unsqueeze(2).to_broadcast([P, HPG, HD]), ALU.mult
                                      ).then_inc(mixed, 1)
                if at in (2, 3):
                    t = at - 2
                    read_done("ssd", g, "cb")
                    dve.wait_ge(exps, 2 * g + t + 1)
                    for h in range(HPG):
                        m = seg[:, s, h, t * P:(t + 1) * P]
                        last = dve.scalar_tensor_tensor(out=m, in0=m, scalar=col[:, 2 + t, h:h + 1], in1=cbm[:, t, :],
                                                        op0=ALU.mult, op1=ALU.mult)
                    last.then_inc(mixed, 1)
                if at == 6:
                    ch.link(dve.tensor_tensor(t_tok[:, :, :].rearrange("p t (h d) -> p t h d", d=HD),
                                              xs[:, :, :].rearrange("p t (h d) -> p t h d", d=HD),
                                              col[:, 6, :].unsqueeze(1).unsqueeze(3).to_broadcast([P, TOK, HPG, HD]),
                                              ALU.mult))
                if at == 8:
                    for t in range(TOK):
                        bank = bank_ready("ssd", g, f"y{t}")
                        dve.tensor_tensor(t_tok[:, t, :], t_tok[:, t, :], spare[:, bank, :], ALU.add
                                          ).then_inc(bank_out[bank], 1)
                if at == 9:
                    bank = bank_ready("ssd", g, "yoff")
                    dve.tensor_tensor(heads_of(x_end[:, :]), heads_of(spare[:, bank, :]),
                                      col[:, 5, :].unsqueeze(2).to_broadcast([P, HPG, HD]), ALU.mult
                                      ).then_inc(bank_out[bank], 1)
                    read_done("ssd", g, "yoff")
                    read_done("ssd", g, "y1")
                    ch.link(dve.tensor_tensor(t_tok[:, 1, :], t_tok[:, 1, :], x_end[:, :], ALU.add))
                if at == 10:
                    pair, use = acc_use("ssd", i, 3 * s + 2)
                    dve.wait_ge(acc_out[pair], use + 1)
                    dve.tensor_tensor(sz[:, :, :], t_tok[:, :, :], sz[:, :, :], ALU.mult).then_inc(gated, 1)
                if at == 13:
                    dve.wait_ge(rms_s, g + 1)
                    ch.link(dve.reciprocal(rms[:, :], rms[:, :]))
                    for t in range(TOK):
                        last = dve.tensor_scalar(sz[:, t, :], sz[:, t, :], rms[:, t:t + 1], None, ALU.mult)
                    last.then_inc(scaled, 1)
                if at == 18:
                    for b, what in enumerate(("ya", "yb")):
                        bank = bank_ready("ssd", g, what)
                        dve.wait_ge(tile_hi, high_no("ssd", g, what) + 1)
                        for k in range(2):
                            ct = 2 * b + k
                            tile = bass.ds(g * TPG + ct, 1)
                            last = dve.scalar_tensor_tensor(out=y_lo[:, tile, :], in0=two_tiles(bank)[:, k:k + 1, :],
                                                            scalar=grp_c[:, s, 30 + ct:31 + ct],
                                                            in1=y_hi[:, tile, :].bitcast(F32),
                                                            op0=ALU.mult, op1=ALU.subtract)
                        last.then_inc(bank_out[bank], 1)

            def convolve(s, jobs, signal):
                seen = [None] * len(jobs)
                for k in range(CONV):
                    back = k
                    for n, (src, dst, at) in enumerate(jobs):
                        tap = grp_c[:, s, at + CONV - 1 - k:at + CONV - k]
                        if k == 0:
                            ins = dve.tensor_scalar(dst, src, tap, grp_c[:, s, at + 4:at + 5], ALU.mult, ALU.add)
                        else:
                            dve.wait_ge(v_seq, seen[n])
                            ins = dve.scalar_tensor_tensor(out=dst[:, back:], in0=src[:, 0:SEQ - back], scalar=tap,
                                                           in1=dst[:, back:], op0=ALU.mult, op1=ALU.add)
                        if k < CONV - 1:
                            seen[n] = ch.mark(ins)
                        elif n == len(jobs) - 1:
                            signal(ins)

            def ssd(i, first):
                for s in range(2):
                    g = i * 2 + s
                    for l in range(24):
                        if not (first and s == 0):
                            ssd_tail(i - 1 + s, 1 - s, g - 1, l)
                        if l in (4, 5):
                            t = l - 4
                            dve.wait_ge(grp, g + 1)
                            dve.wait_ge(seg_in[s], 16 * (i + 1))
                            for h in range(HPG):
                                m = seg[:, s, h, t * P:(t + 1) * P]
                                last = dve.tensor_scalar(m, m, grp_d[:, s, t, h:h + 1], 0.0, ALU.subtract, ALU.min)
                            last.then_inc(args, 1)
                        if l in (14, 16):
                            b = (l - 14) // 2
                            bank = bank_ready("ssd", g, "xa" if b == 0 else "xb")
                            use = spare_use("ssd", g, "xa" if b == 0 else "xb")[1]

                            def done(ins, bank=bank, use=use, b=b):
                                ins.then_inc(bank_out[bank], 1)
                                if b == 1:
                                    dve.wait_ge(bank_out[bank], use + 1)

                            convolve(s, [(two_tiles(bank)[:, k, :], conv[:, 2 * b + k, :], 5 * (2 * b + k))
                                         for k in range(2)], done)
                        if l == 21:
                            bank = bank_ready("ssd", g, "bc")
                            convolve(s, [(two_tiles(bank)[:, k, :], bcT[:, k, :], 20 + 5 * k) for k in range(2)],
                                     lambda ins, bank=bank: ins.then_inc(bank_out[bank], 1))
                        split("ssd", i, s * 24 + l, W if l // 8 != 1 else 2 * NS)

            ssd(0, True)
            with dve.Fori(1, GROUPS // 2) as i:
                ch.enter(i, 1, SSD_LINKS)
                ssd(i, False)
                ch.leave(GROUPS // 2)

            def merged(u):
                pair, use = acc_use("merge", u, 0)
                dve.wait_ge(acc_out[pair], use + 1)
                pair, y_s = acc_ready("merge", u, 1)
                dve.scalar_tensor_tensor(out=sz[:, :, :], in0=sz[:, :, :], scalar=1.0, in1=y_s, op0=ALU.add,
                                         op1=ALU.mult).then_inc(acc_out[pair], 1)
                _, use = acc_use("merge", u, 1)
                dve.wait_ge(acc_out[pair], use + 1)
                dve.tensor_tensor(sz[:, :, :], sz[:, :, :], gate_a[:, :, bass.ds(u * W, W)], ALU.add
                                  ).then_inc(gated, 1)

            def merge(i, first):
                for l in range(24):
                    if first:
                        ssd_tail(GROUPS // 2 - 1, 1, GROUPS - 1, l)
                    elif l == 2:
                        merged(i - 1)
                    elif l == 7:
                        rest_tiles("merge", i - 1, ("ma", "mb"), o_hi, o_lo, (i - 1) * 4, 0.5)
                    split("merge", i, l)

            merge(0, True)
            with dve.Fori(1, NC_D) as i:
                merge(i, False)
            for l in range(32):
                if l == 2:
                    merged(NC_D - 1)
                if l == 6:
                    rest_tiles("merge", NC_D - 1, ("ma", "mb"), o_hi, o_lo, (NC_D - 1) * 4, 0.5)
                if l % 8 == 7:
                    c = l // 8
                    prepare_rows(1, c)
                if l % 8 == 2 and l > 8:
                    c = l // 8 - 1
                    evacuate("out", 0, c, c, 1.0)
                split("out", 0, l)
            evacuate("out", 0, NC_D - 1, NC_D - 1, 1.0)
            normalise(2)
            ln_chunk(0)
            ln_chunk(1)
            ffn(2, "ln2", 2)
            normalise(3)
            dve.scalar_tensor_tensor(out=shift[:, :], in0=mv[:, :, 0], scalar=-1.0, in1=rstd[:, :], op0=ALU.mult,
                                     op1=ALU.mult).then_inc(ln_x, 1)
            dve.wait_ge(last_rows_in, 32)
            for c in range(NC_D):
                dve.wait_ge(normed, c + 1)
                part = resid[:, :, c * W:(c + 1) * W]
                gain = last_rows[:, 0:1, c * W:(c + 1) * W].to_broadcast([P, TOK, W])
                bias = last_rows[:, 1:2, c * W:(c + 1) * W].to_broadcast([P, TOK, W])
                ch.link(dve.tensor_tensor(part, part, gain, ALU.mult))
                dve.tensor_tensor(part, part, bias, ALU.add).then_inc(ln_x, 1)


NAMES = ["x", "positions", "ffn1_w_gate", "ffn1_w_up", "ffn1_w_down", "ln1_g", "ln1_b", "w_in", "conv_w", "conv_b",
         "dt_bias", "a_log", "d_skip", "ssd_norm_g", "w_ssd_o", "attn_sinks", "w_attn_o", "w_out", "ln2_g", "ln2_b",
         "ffn2_w_gate", "ffn2_w_up", "ffn2_w_down", "ln3_g", "ln3_b"]


def kernel(**inputs):
    import concourse.bacc as bacc
    from concourse.bass_utils import run_bass_kernel_spmd

    nc = bacc.Bacc("TRN2", target_bir_lowering=False, num_devices=1)
    arrays, args = {}, []
    for name in NAMES:
        a = np.ascontiguousarray(inputs[name])
        arrays[name] = a
        args.append(nc.dram_tensor(name, a.shape, mybir.dt.from_np(a.dtype), kind="ExternalInput").ap())
    args.append(nc.dram_tensor("acs_rows", (HEADS, SEQ), F32, kind="Internal").ap())
    args.append(nc.dram_tensor("kept", (SEQ, D), F32, kind="Internal").ap())
    args.append(nc.dram_tensor("out", (1, SEQ, D), F32, kind="ExternalOutput").ap())
    build_decoder_layer(nc, *args)
    r = run_bass_kernel_spmd(nc, [arrays], core_ids=[0])
    return r.results[0]["out"]
```

```python
from contextlib import ExitStack

import numpy as np

import concourse.bass as bass
from concourse import mybir

F32 = mybir.dt.float32
F32R = mybir.dt.float32r
I32 = mybir.dt.int32
ALU = mybir.AluOpType
ACT = mybir.ActivationFunctionType
AX = mybir.AxisListType

P = 128
SEQ = 256
TOK = SEQ // P
D = 2048
KD = D // P
F = 5632
KF = F // P
W = 512
NC_D = D // W
NC_F = F // W
DI = 4096
KI = DI // P
HEADS = 64
HD = 64
GROUPS = 8
HPG = HEADS // GROUPS
TPG = W // P
NS = 128
XBC = DI + 2 * GROUPS * NS
KX = XBC // P
CONV = 4
QH = 32
KVH = 4
QPK = QH // KVH
HALF = HD // 2
THETA = 10000.0
ALPHA = 2.0 ** 0.25
EPS = 1e-5
MASKED = -1e30

Z0 = 0
X0 = DI
B0 = X0 + DI
C0 = B0 + GROUPS * NS
DT0 = X0 + XBC
Q0 = DT0 + HEADS
K0 = Q0 + D
V0 = K0 + KVH * HD
GS0 = V0 + KVH * HD
GA0 = GS0 + D

SHARED_WAITS = (("ssd", 16), ("merge", 8))
ATTN_O_ORDER = ([(c, k) for c in range(2) for k in range(6)] + [(c, k) for c in range(2) for k in (6, 7)],
                [(c, k) for c in range(2) for k in range(8)])
LAST_UNIT = [(0, 1), (2,), (3,), (4,), (5,), (6, 7), (8,), (9,), (10,), (11,), (12, 13), (14, 15), (), (), (), ()]
POOL_BIASES = 2
EARLY = 3
LAND = 4
SPLIT = 4

PHASES = {
    "up1": (NC_F, [(8, 0), (8, 1)]),
    "down1": (2, [(22, 0), (22, 1)]),
    "kvdt": (1, [(8, 0), (8, 1)]),
    "attn": (KVH, [(8, 0), (8, 1)]),
    "attn_o": (2, [(8, 0), (8, 1)]),
    "ssd": (GROUPS // 2, [(8, 0), (8, 1), (8, 0), (8, 1), (8, 0), (8, 1)]),
    "merge": (NC_D, [(8, 0), (16, 1)]),
    "out": (1, [(8, 0), (8, 1), (8, 0), (8, 1)]),
    "up2": (NC_F, [(8, 0), (8, 1)]),
    "down2": (2, [(22, 0), (22, 1)]),
}
LN_USES = [(f"t{u}", u % 4) for u in range(8)]
SPARE = {
    "xT": (1, LN_USES),
    "up1": (NC_F, [("ga", 0), ("gb", 1)]),
    "ln1": (1, LN_USES),
    "prep": (1, [("ka", 0), ("kb", 1), ("raw", 2), ("acs", 2), ("rows", 3)]),
    "attn": (KVH, [("qa", 0), ("qb", 1)] + [(f"s{h}", h % 4) for h in range(QPK)]
             + [(f"p{h}", h % 4) for h in range(QPK)] + [("o0", 0), ("o1", 1), ("oa", 2), ("ob", 3)]),
    "ssd": (GROUPS, [("xa", 0), ("xb", 1), ("bc", 2), ("x0", 0), ("x1", 1), ("cb", 3),
                     ("st", 2), ("y0", 0), ("y1", 1), ("yoff", 3), ("ya", 2), ("yb", 3)]),
    "merge": (NC_D, [("ma", 0), ("mb", 1)]),
    "ln2": (1, LN_USES),
    "up2": (NC_F, [("ga", 0), ("gb", 1)]),
}
SPLIT_USES = {"xT": LN_USES, "up1": SPARE["up1"][1], "ln1": LN_USES, "attn": [("oa", 2), ("ob", 3)],
              "ssd": [("ya", 2), ("yb", 3)], "merge": SPARE["merge"][1], "ln2": LN_USES, "up2": SPARE["up2"][1]}
DEC_V = 4
ATTN_LINKS = 8
SSD_LINKS = 2 * (1 + 3 * 2 * (CONV - 2))


def slab_bases():
    base, at = {}, 0
    for name, (n, chunks) in PHASES.items():
        per = sum(c[0] for c in chunks)
        base[name] = (at, per)
        at += n * per
    return base


SLABS = slab_bases()


def slab_no(phase, i, l):
    return SLABS[phase][0] + i * SLABS[phase][1] + l


def loads(phase, i, l):
    base, per = SLABS[phase]
    n = base // LAND + i * (per // LAND) + l // LAND + 1
    double = 8 // LAND
    if base > SLABS["ssd"][0]:
        n = n + GROUPS * double
    if phase == "ssd":
        n = n + i * (2 * double) + sum(m % 24 // 8 == 1 for m in range(l % LAND, l + 1, LAND))
    return n


def acc_use(phase, i, c):
    pair = PHASES[phase][1][c][1]
    at = 0
    for name, (n, chunks) in PHASES.items():
        per = sum(q == pair for _, q in chunks)
        if name == phase:
            return pair, at + i * per + sum(q == pair for _, q in chunks[:c])
        at += n * per


def spare_use(phase, u, what):
    names = [w for w, _ in SPARE[phase][1]]
    k = names.index(what)
    bank = SPARE[phase][1][k][1]
    at = 0
    for name, (n, uses) in SPARE.items():
        per = sum(b == bank for _, b in uses)
        if name == phase:
            return bank, at + u * per + sum(b == bank for _, b in uses[:k])
        at += n * per


def high_no(phase, u, what):
    at = 0
    for name, uses in SPLIT_USES.items():
        if name == phase:
            return at + u * len(uses) + [w for w, _ in uses].index(what)
        at += SPARE[name][0] * len(uses)


class Chain:

    def __init__(self, eng, sem):
        self.eng, self.sem, self.base, self.i, self.per, self.k = eng, sem, 0, 0, 0, 0

    def enter(self, i, first, per):
        self.base += self.k
        self.i, self.per, self.first, self.k = i, per, first, 0

    def leave(self, end):
        assert self.k == self.per, f"an iteration counts {self.k}"
        self.base, self.i, self.k = self.base + self.per * (end - self.first), 0, 0
        self.per = 0

    def now(self):
        if self.per:
            return self.base - self.first * self.per + self.k + self.i * self.per
        return self.base + self.k

    def link(self, ins):
        ins.then_inc(self.sem, 1)
        self.k += 1
        self.eng.wait_ge(self.sem, self.now())

    def mark(self, ins):
        ins.then_inc(self.sem, 1)
        self.k += 1
        return self.now()


def two_pi_parts():
    whole = 2 * np.pi
    a = np.floor(whole * 2.0 ** 9) / 2.0 ** 9
    b = np.floor((whole - a) * 2.0 ** 21) / 2.0 ** 21
    return float(a), float(b), float(np.float32(whole - a - b))


def build_decoder_layer(nc, x, positions, ffn1_w_gate, ffn1_w_up, ffn1_w_down, ln1_g, ln1_b, w_in, conv_w, conv_b,
                        dt_bias, a_log, d_skip, ssd_norm_g, w_ssd_o, attn_sinks, w_attn_o, w_out, ln2_g, ln2_b,
                        ffn2_w_gate, ffn2_w_up, ffn2_w_down, ln3_g, ln3_b, acs_rows, kept, out):
    ctx = ExitStack()

    def sb(name, shape, dt=F32):
        return ctx.enter_context(nc.sbuf_tensor(name, shape, dt))

    def sem(name):
        return ctx.enter_context(nc.semaphore(name))

    def tiles(w):
        return w[0].rearrange("(k p) n -> p k n", p=P)

    win, wso, wao, wou = tiles(w_in), tiles(w_ssd_o), tiles(w_attn_o), tiles(w_out)
    ffn_w = {1: (tiles(ffn1_w_gate), tiles(ffn1_w_up), tiles(ffn1_w_down)),
             2: (tiles(ffn2_w_gate), tiles(ffn2_w_up), tiles(ffn2_w_down))}
    x_view = x[0].rearrange("(t p) n -> p t n", p=P)
    kept_view = kept.rearrange("(t p) n -> p t n", p=P)
    out_view = out[0].rearrange("(t p) n -> p t n", p=P)

    with ctx:
        land = sb("land", [P, LAND, 2, W])
        w_hi = sb("w_hi", [P, SPLIT, 2, W], F32R)
        w_lo = sb("w_lo", [P, SPLIT, 2, W], F32R)
        resid = sb("resid", [P, TOK, D])
        gate_a = resid
        silu_t = resid[:, :, 0:W]
        prod = resid[:, :, W:2 * W]
        at0 = -(-nc.sbuf_base // 32) * 32
        sb("region", [P, 32 * 1024])

        def placed(name, shape, dt, at):
            return nc.alloc_sbuf_tensor_at(name, shape, dt, offset=at0 + at)

        K = 1024
        a_hi = placed("a_hi", [P, KD, SEQ], F32R, 96 * K)
        a_lo = placed("a_lo", [P, KD, SEQ], F32R, 112 * K)
        rows = placed("rows", [P, 2, D], F32, 96 * K)
        last_rows = placed("last_rows", [P, 2, D], F32, 112 * K)
        g_hi = placed("g_hi", [P, KF, SEQ], F32R, 0)
        g_lo = placed("g_lo", [P, KF, SEQ], F32R, 44 * K)
        y_hi = placed("y_hi", [P, KI, SEQ], F32R, 0)
        y_lo = placed("y_lo", [P, KI, SEQ], F32R, 32 * K)
        o_hi = placed("o_hi", [P, KD, SEQ], F32R, 64 * K)
        o_lo = placed("o_lo", [P, KD, SEQ], F32R, 80 * K)
        s_sb = placed("s_sb", [P, QPK, 3 * P], F32, 0)
        pT = placed("pT", [P, QPK, 3 * P], F32, 12 * K)
        qT = placed("qT", [P, TPG, SEQ], F32, 24 * K)
        q_rot = placed("q_rot", [P, TOK, W], F32, 28 * K)
        rot = placed("rot", [P, 4, W], F32, 32 * K)
        kT = placed("kT", [P, KVH, SEQ], F32, 40 * K)
        v_all = placed("v_all", [P, TOK, KVH * HD], F32, 44 * K)
        kT_j = placed("kT_j", [P, SEQ], F32, 46 * K)
        v_j = placed("v_j", [P, TOK, HD], F32, 47 * K)
        o_tok = placed("o_tok", [P, TOK, W], F32, 48 * K)
        k_rot = placed("k_rot", [P, TOK, KVH, 2, HD], F32, 52 * K)
        soft = placed("soft", [P, 64], F32, 56 * K)
        spl = placed("spl", [P, 6, TOK * HEADS], F32, 57 * K)
        rows_sb = placed("rows_sb", [HEADS, SEQ], F32, 60 * K)
        head_r = placed("head_r", [P, 3, HEADS], F32, 61 * K)
        seg = placed("seg", [P, 2, HPG, SEQ], F32, 64 * K)
        u_tok = placed("u_tok", [P, TOK, W], F32, 80 * K)
        conv = placed("conv", [P, TPG, SEQ], F32, 84 * K)
        t_tok = placed("t_tok", [P, TOK, W], F32, 84 * K)
        xs = placed("xs", [P, TOK, W], F32, 88 * K)
        x_end = placed("x_end", [P, W], F32, 92 * K)
        state = placed("state", [P, W], F32, 94 * K)
        sz = sb("sz", [P, TOK, W])
        bcT = sb("bcT", [P, 2, SEQ])
        b_tok = sb("b_tok", [P, P])
        cbm = sb("cbm", [P, TOK, P])
        ident = sb("ident", [P, P])
        upper = sb("upper", [P, P])
        ones = sb("ones", [P, P])
        mask = sb("mask", [P, 3 * P])
        vec_c = sb("vec_c", [P, GROUPS, 34])
        vec_d = sb("vec_d", [P, GROUPS, 7, HPG])
        grp_c = sb("grp_c", [P, 2, 34])
        grp_d = sb("grp_d", [P, 2, 7, HPG])
        ln_col = sb("ln_col", [P, 4, KD])
        sink_r = sb("sink_r", [P, QH])
        cosr = sb("cosr", [P, TOK, HALF])
        sinr = sb("sinr", [P, TOK, HALF])
        stats = sb("stats", [P, TOK, NC_D, 6])
        mv = sb("mv", [P, TOK, 2])
        rstd = sb("rstd", [P, TOK])
        shift = sb("shift", [P, TOK])
        rms = sb("rms", [P, TOK])
        eps = sb("eps", [P, 1])
        minus_half = sb("minus_half", [P, 1])
        half_pi = sb("half_pi", [P, 1])
        par = placed("par", [P, 4, P], F32, 0)
        inv_f = placed("inv_f", [P, HALF], F32, 4 * K)
        pos_i = placed("pos_i", [P, TOK], I32, 5 * K)
        pos_f = placed("pos_f", [P, TOK], F32, 5 * K + 64)
        ang = placed("ang", [P, 6, TOK * HALF], F32, 6 * K)

        acc = ctx.enter_context(nc.psum_tensor("acc", [P, 4, W], F32))
        spare = ctx.enter_context(nc.psum_tensor("spare", [P, 4, W], F32))

        landed = [sem(f"landed{r}") for r in range(LAND)]
        high = sem("high")
        rest = sem("rest")
        used = sem("used")
        acc_out = [sem(f"acc_out{p}") for p in range(2)]
        bank_in = [sem(f"bank_in{b}") for b in range(4)]
        bank_out = [sem(f"bank_out{b}") for b in range(4)]
        tile_hi = sem("tile_hi")
        v_seq = sem("v_seq")
        s_seq = sem("s_seq")
        p_seq = sem("p_seq")
        x_in = [sem(f"x_in{c}") for c in range(NC_D)]
        par_in = sem("par_in")
        row_in = sem("row_in")
        pos_in = sem("pos_in")
        setup = sem("setup")
        par_t = sem("par_t")
        trig = sem("trig")
        trig_s = sem("trig_s")
        dec_v = sem("dec_v")
        dec_s = sem("dec_s")
        v_kept = sem("v_kept")
        k_rotated = sem("k_rotated")
        rows_out = sem("rows_out")
        seg_in = [sem(f"seg_in{s}") for s in range(2)]
        apart = sem("apart")
        args = sem("args")
        exps = sem("exps")
        mixed = sem("mixed")
        silu_x = sem("silu_x")
        silu_bc = sem("silu_bc")
        b_out = sem("b_out")
        gated = sem("gated")
        squared = sem("squared")
        scaled = sem("scaled")
        maxed = sem("maxed")
        prob = sem("prob")
        q_rotated = sem("q_rotated")
        kv_copy = sem("kv_copy")
        weighed = sem("weighed")
        taps = sem("taps")
        rms_p = sem("rms_p")
        ln_v = sem("ln_v")
        ln_p = sem("ln_p")
        ln_x = sem("ln_x")
        gained = sem("gained")
        biased = sem("biased")
        normed = sem("normed")
        rows_in = sem("rows_in")
        last_rows_in = sem("last_rows_in")
        resid_in = sem("resid_in")
        kept_out = sem("kept_out")
        stored = sem("stored")

        block = ctx.enter_context(nc.Block())

        @block.sync
        def _(sp):
            def load(phase, i, l, *sources, width=W):
                n = slab_no(phase, i, l)
                if not (phase == "up1" and isinstance(i, int) and n < LAND):
                    if (phase, l + 1) in SHARED_WAITS:
                        sp.wait_ge(rest, n - LAND + 2)
                    elif (phase, l) not in SHARED_WAITS:
                        sp.wait_ge(rest, n - LAND + 1)
                part = width // len(sources)
                for k, src in enumerate(sources):
                    sp.dma_start(land[:, l % LAND, :, k * part:(k + 1) * part], src).then_inc(landed[l % LAND], 16)

            def up(f, phase, i, x_before={}):
                for l in range(16):
                    if l in x_before:
                        first_x(x_before[l])
                    k = 2 * (l % 8)
                    load(phase, i, l, ffn_w[f][l // 8][:, k:k + 2, bass.ds(i * W, W)])

            def down(f, phase):
                with sp.Fori(0, 2) as j:
                    for l in range(44):
                        c, k = l // 22, 2 * (l % 22)
                        load(phase, j, l, ffn_w[f][2][:, k:k + 2, bass.ds(j * 2 * W + c * W, W)])

            def first_x(c):
                sp.dma_start(resid[:, :, c * W:(c + 1) * W], x_view[:, :, c * W:(c + 1) * W]).then_inc(x_in[c], 16)

            first_x(0)
            up(1, "up1", 0, {1: 1, 3: 2, 5: 3})
            with sp.Fori(1, NC_F) as i:
                up(1, "up1", i)
            down(1, "down1")
            for l in range(16):
                k = 2 * (l % 8)
                if l < 8:
                    load("kvdt", 0, l, win[:, k:k + 2, K0:K0 + W])
                else:
                    load("kvdt", 0, l, win[:, k:k + 2, DT0:DT0 + HEADS], width=HEADS)
            with sp.Fori(0, KVH) as j:
                for l in range(16):
                    k = 2 * (l % 8)
                    load("attn", j, l, win[:, k:k + 2, bass.ds(j * W + (Q0 if l < 8 else GA0), W)])
            for j in range(2):
                for l, (c, slab) in enumerate(ATTN_O_ORDER[j]):
                    at = (2 * j + c) * W
                    load("attn_o", j, l, wao[:, 2 * slab:2 * slab + 2, at:at + W])
            with sp.Fori(0, GROUPS // 2) as i:
                for s in range(2):
                    for l in range(24):
                        k = 2 * (l % 8)
                        if l // 8 == 1:
                            load("ssd", i, s * 24 + l, *(win[:, k:k + 2, bass.ds(i * 2 * NS + (c + s * NS), NS)]
                                                         for c in (B0, C0)), width=2 * NS)
                        else:
                            c = (X0 if l < 8 else Z0) + s * W
                            load("ssd", i, s * 24 + l, win[:, k:k + 2, bass.ds(i * 2 * W + c, W)])
            with sp.Fori(0, NC_D) as i:
                for l in range(24):
                    if l < 8:
                        load("merge", i, l, win[:, 2 * l:2 * l + 2, bass.ds(i * W + GS0, W)])
                    else:
                        k = 2 * (l - 8)
                        load("merge", i, l, wso[:, k:k + 2, bass.ds(i * W, W)])
            for l in range(32):
                c, k = l // 8, 2 * (l % 8)
                load("out", 0, l, wou[:, k:k + 2, c * W:(c + 1) * W])
            with sp.Fori(0, NC_F) as i:
                up(2, "up2", i)
            down(2, "down2")
            sp.wait_ge(stored, 16 * NC_D)

        @block.gpsimd
        def _(pool):
            ch = Chain(pool, p_seq)
            ch.link(pool.memset(ident[:, :], 0.0))
            ch.link(pool.affine_select(out=ident[:, :], in_=ident[:, :], compare_op=ALU.not_equal, fill=1.0,
                                       base=0, pattern=[[-1, P]], channel_multiplier=1))
            pool.memset(eps[:, :], EPS)
            pool.memset(minus_half[:, :], -0.5)
            pool.memset(half_pi[:, :], float(np.pi / 2))
            inv_freq = (THETA ** (-np.arange(HALF) * 2.0 / HD)).astype(np.float32)
            for k in range(HALF):
                pool.memset(inv_f[:, k:k + 1], float(inv_freq[k]))
            pool.memset(ones[:, :], 1.0)
            pool.memset(upper[:, :], 1.0)
            ch.link(pool.memset(mask[:, :], 0.0))
            pool.affine_select(out=upper[:, :], in_=upper[:, :], compare_op=ALU.is_ge, fill=0.0,
                               base=0, pattern=[[1, P]], channel_multiplier=-1)
            for b in range(3):
                m = mask[:, b * P:(b + 1) * P]
                if b == 1:
                    last = pool.affine_select(out=m, in_=m, compare_op=ALU.is_gt, fill=MASKED,
                                              base=0, pattern=[[1, P]], channel_multiplier=-1)
                else:
                    last = pool.affine_select(out=m, in_=m, compare_op=ALU.is_ge, fill=MASKED,
                                              base=0, pattern=[[-1, P]], channel_multiplier=1)
            last.then_inc(setup, 1)
            for src, q, r in ((conv_w[0, 0:2, :].rearrange("j (t p) -> (j t) p", p=P), 0, 0),
                              (conv_w[0, 2:4, :].rearrange("j (t p) -> (j t) p", p=P), 1, 0),
                              (conv_b[0].rearrange("(t p) -> t p", p=P), 2, 0),
                              (ssd_norm_g[0].rearrange("(t p) -> t p", p=P), 2, KX),
                              (ln1_g[0].rearrange("(t p) -> t p", p=P), 3, 0),
                              (ln1_b[0].rearrange("(t p) -> t p", p=P), 3, KD),
                              (ln2_g[0].rearrange("(t p) -> t p", p=P), 3, 2 * KD),
                              (ln2_b[0].rearrange("(t p) -> t p", p=P), 3, 3 * KD)):
                pool.dma_start(par[r:r + src.shape[0], q, :], src).then_inc(par_in, 16)
            for t in range(TOK):
                pool.dma_start(pos_i[:, t:t + 1], positions[0, t * P:(t + 1) * P].unsqueeze(1)).then_inc(pos_in, 16)
            pool.dma_start(sink_r[:, :], attn_sinks[0].partition_broadcast(P)).then_inc(pos_in, 16)
            def load_rows(dst, gain, bias, arrived):
                pool.dma_start(dst[:, 0, :], gain[0, :].partition_broadcast(P)).then_inc(arrived, 16)
                pool.dma_start(dst[:, 1, :], bias[0, :].partition_broadcast(P)).then_inc(arrived, 16)

            def hidden_complete(phase):
                bank, use = spare_use(phase, NC_F - 1, "gb")
                pool.wait_ge(bank_in[bank], use + 1)

            def reciprocal_root(dst, src):
                ch.link(pool.tensor_tensor(dst, src, eps[:, :].to_broadcast([P, TOK]), ALU.add))
                return pool.tensor_tensor(dst, dst, minus_half[:, :].to_broadcast([P, TOK]), ALU.pow)

            def deviations(no):
                pool.wait_ge(ln_v, no)
                reciprocal_root(rstd[:, :], mv[:, :, 1]).then_inc(ln_p, 1)

            def keep_stream(first):
                for c in range(NC_D):
                    pool.wait_ge(ln_x, first + c + 1)
                    pool.dma_start(kept_view[:, :, c * W:(c + 1) * W], resid[:, :, c * W:(c + 1) * W]
                                   ).then_inc(kept_out, 16)

            hidden_complete("up1")
            pool.dma_start(resid[:, :, :], x_view).then_inc(resid_in, 16)
            deviations(1)
            keep_stream(0)
            with pool.Fori(0, KVH) as j:
                bank, use = spare_use("prep", 0, "kb")
                pool.wait_ge(bank_out[bank], use + 1)
                bank, use = spare_use("attn", j - 1, "s7")
                pool.wait_ge(bank_in[bank], use + 1)
                pool.tensor_copy(kT_j[:, :], kT[:, bass.ds(j, 1), :].rearrange("p a n -> p (a n)")).then_inc(kv_copy, 1)
                bank, use = spare_use("attn", j - 1, "o1")
                pool.wait_ge(bank_in[bank], use + 1)
                pool.tensor_copy(v_j[:, :, :], v_all[:, :, bass.ds(j * HD, HD)]).then_inc(kv_copy, 1)
            pool.wait_ge(dec_v, DEC_V)
            pool.wait_ge(rows_out, 16)
            pool.wait_ge(used, slab_no("attn_o", 1, 15) + 1)

            def from_tokens(g, s):
                for t in range(TOK):
                    bank, use = spare_use("ssd", g, f"x{t}")
                    pool.wait_ge(bank_out[bank], use + 1)
                pool.tensor_tensor(x_end[:, :].rearrange("p (h d) -> p h d", d=HD),
                                   xs[:, 0, :].rearrange("p (h d) -> p h d", d=HD),
                                   grp_d[:, s, 4, :].unsqueeze(2).to_broadcast([P, HPG, HD]), ALU.mult
                                   ).then_inc(weighed, 1)
                pool.tensor_tensor(t_tok[:, :, :].rearrange("p t (h d) -> p t h d", d=HD),
                                   xs[:, :, :].rearrange("p t (h d) -> p t h d", d=HD),
                                   grp_d[:, s, 6, :].unsqueeze(1).unsqueeze(3).to_broadcast([P, TOK, HPG, HD]), ALU.mult
                                   ).then_inc(weighed, 1)

            def roots(g):
                pool.wait_ge(squared, g + 1)
                reciprocal_root(rms[:, :], rms[:, :]).then_inc(rms_p, 1)

            def ssd(i, first):
                for s in range(2):
                    g = i * 2 + s
                    bank, use = spare_use("ssd", g - 2, "yb")
                    pool.wait_ge(bank_out[bank], use + 1)
                    pool.dma_start(seg[:, s, :, :], acs_rows[bass.ds(g * HPG, HPG), :].partition_broadcast(P)
                                   ).then_inc(seg_in[s], 16)
                    pool.tensor_copy(grp_c[:, s, :], vec_c[:, bass.ds(g, 1), :].rearrange("p a n -> p (a n)"))
                    ch.link(pool.tensor_copy(grp_d[:, s, :, :],
                                             vec_d[:, bass.ds(g, 1), :, :].rearrange("p a b n -> p (a b) n")))
                    if not (first and s == 0):
                        from_tokens(g - 1, 1 - s)
                    pool.wait_ge(seg_in[s], 16 * (i + 1))
                    for t in range(TOK):
                        m = seg[:, s, :, t * P:(t + 1) * P]
                        pool.tensor_tensor(m, m, grp_d[:, s, t, :].unsqueeze(2).to_broadcast([P, HPG, P]),
                                           ALU.subtract).then_inc(apart, 1)
                    if not (first and s == 0):
                        roots(g - 1)

            ssd(0, True)
            with pool.Fori(1, GROUPS // 2) as i:
                ch.enter(i, 1, 4)
                ssd(i, False)
                ch.leave(GROUPS // 2)
            from_tokens(GROUPS - 1, 1)
            roots(GROUPS - 1)
            pool.wait_ge(used, slab_no("merge", NC_D - 1, 7) + 1)
            load_rows(rows, ln1_g, ln1_b, rows_in)
            pool.wait_ge(gated, GROUPS + NC_D)
            pool.wait_ge(kept_out, 16 * NC_D)
            pool.dma_start(resid[:, :, :], kept_view).then_inc(resid_in, 16)
            deviations(2)
            keep_stream(NC_D)
            pool.wait_ge(used, slab_no("up2", NC_F - 1, 15) + 1)
            hidden_complete("up2")
            pool.wait_ge(kept_out, 2 * 16 * NC_D)
            pool.dma_start(resid[:, :, :], kept_view).then_inc(resid_in, 16)
            pool.wait_ge(used, slab_no("down2", 0, 8))
            load_rows(rows, ln2_g, ln2_b, rows_in)
            pool.wait_ge(used, slab_no("down2", 0, 24))
            load_rows(last_rows, ln3_g, ln3_b, last_rows_in)
            deviations(3)
            for c in range(POOL_BIASES):
                pool.wait_ge(gained, c + 1)
                part = resid[:, :, c * W:(c + 1) * W]
                pool.tensor_tensor(part, part, last_rows[:, 1:2, c * W:(c + 1) * W].to_broadcast([P, TOK, W]), ALU.add
                                   ).then_inc(biased, 1)

        @block.tensor
        def _(pe):
            def free_bank(phase, u, what):
                bank, use = spare_use(phase, u, what)
                if not (isinstance(use, int) and use == 0):
                    pe.wait_ge(bank_out[bank], use)
                return bank

            def wait_bank(phase, u, what):
                bank, use = spare_use(phase, u, what)
                pe.wait_ge(bank_out[bank], use + 1)

            def turn(bank, at, src, rows=P):
                return pe.transpose(spare[0:src.shape[-1], bank, at:at + rows], src, ident[0:rows, 0:rows])

            def turn_rows(phase, u, names, src):
                for b, what in enumerate(names):
                    bank = free_bank(phase, u, what)
                    for k in range(2):
                        for t in range(TOK):
                            c = (2 * b + k) * P
                            last = turn(bank, k * SEQ + t * P, src[:, t, c:c + P])
                    last.then_inc(bank_in[bank], 1)

            def slab(phase, i, c, s, a, b, width=W, at=None):
                chunks = PHASES[phase][1]
                l = sum(n for n, _ in chunks[:c]) + s if at is None else at
                n_slabs = chunks[c][0]
                if s == 0:
                    pair, use = acc_use(phase, i, c)
                    if not (isinstance(use, int) and use == 0):
                        pe.wait_ge(acc_out[pair], use)
                pair = chunks[c][1]
                pe.wait_ge(rest, slab_no(phase, i, l) + 1)
                for k in range(2):
                    first, last = s == 0 and k == 0, s == n_slabs - 1 and k == 1
                    for t in range(TOK):
                        to = acc[:, 2 * pair + t, 0:width]
                        rows_hi = a[:, 2 * s + k, t * P:(t + 1) * P]
                        rows_lo = b[:, 2 * s + k, t * P:(t + 1) * P]
                        hi, lo = w_hi[:, l % SPLIT, k, 0:width], w_lo[:, l % SPLIT, k, 0:width]
                        pe.matmul(to, rows_hi, hi, start=first, stop=False)
                        pe.matmul(to, rows_hi, lo, start=False, stop=False)
                        mm = pe.matmul(to, rows_lo, hi, start=False, stop=last)
                mm.then_inc(used, 1)

            def ln_turn(phase, u, x_no):
                bank = free_bank(phase, 0, f"t{u}")
                if x_no is None:
                    pe.wait_ge(x_in[u // 2], 16)
                elif u % 2 == 0:
                    pe.wait_ge(ln_x, x_no + u // 2 + 1)
                for k in range(2):
                    for t in range(TOK):
                        c = (2 * u + k) * P
                        last = turn(bank, k * SEQ + t * P, resid[:, t, c:c + P])
                last.then_inc(bank_in[bank], 1)

            def up(phase, i, first, ln, x_no):
                for l in range(16):
                    if first and l < 8:
                        wait_bank(ln, 0, f"t{l}")
                    if phase == "up1" and first and l == 6:
                        pe.wait_ge(par_in, 16 * 8)
                        for q, rows in enumerate((2 * KX, 2 * KX, KX + KI, 4 * KD)):
                            last = pe.transpose(acc[:, 2, q * P:q * P + rows], par[0:rows, q, :], ident[0:rows, 0:rows])
                        last.then_inc(par_t, 1)
                    if phase == "up1" and first and l == 8:
                        pe.wait_ge(dec_v, 1)
                    if not first and l == 4:
                        up_turn(phase, i - 1)
                    slab(phase, i, l // 8, l % 8, a_hi, a_lo)
                    if first and l + 4 < 8:
                        ln_turn(ln, l + 4, x_no)

            def up_turn(phase, u):
                pair, use = acc_use(phase, u, 1)
                pe.wait_ge(acc_out[pair], use + 1)
                turn_rows(phase, u, ("ga", "gb"), prod)

            def ffn(f, ln, x_no):
                phase = f"up{f}"
                for u in range(4):
                    ln_turn(ln, u, x_no)
                up(phase, 0, True, ln, x_no)
                with pe.Fori(1, NC_F) as i:
                    up(phase, i, False, ln, x_no)
                for j in range(2):
                    for l in range(44):
                        if j == 0 and l == 2:
                            up_turn(phase, NC_F - 1)
                        if j == 0 and l == 20:
                            wait_bank(phase, NC_F - 1, "ga")
                            wait_bank(phase, NC_F - 1, "gb")
                        slab(f"down{f}", j, l // 22, l % 22, g_hi, g_lo)

            pe.wait_ge(p_seq, 2)
            ffn(1, "xT", None)

            def slab_of_heads(s):
                l = PHASES["kvdt"][1][0][0] + s
                pair, use = acc_use("kvdt", 0, 1)
                if s == 0:
                    pe.wait_ge(acc_out[pair], use)
                pe.wait_ge(rest, slab_no("kvdt", 0, l) + 1)
                to = acc[0:HEADS, 2 * pair, 0:SEQ]
                for k in range(2):
                    hi, lo = w_hi[:, l % SPLIT, k, 0:HEADS], w_lo[:, l % SPLIT, k, 0:HEADS]
                    pe.matmul(to, hi, a_hi[:, 2 * s + k, :], start=s == 0 and k == 0, stop=False)
                    pe.matmul(to, hi, a_lo[:, 2 * s + k, :], start=False, stop=False)
                    mm = pe.matmul(to, lo, a_hi[:, 2 * s + k, :], start=False, stop=s == 7 and k == 1)
                mm.then_inc(used, 1)

            for u in range(4):
                ln_turn("ln1", u, 0)
            for l in range(16):
                if l < 8:
                    wait_bank("ln1", 0, f"t{l}")
                if l < 8:
                    slab("kvdt", 0, 0, l, a_hi, a_lo)
                else:
                    slab_of_heads(l - 8)
                if l + 4 < 8:
                    ln_turn("ln1", l + 4, 0)

            def scores(j, heads):
                if 0 in heads:
                    pe.wait_ge(kv_copy, 2 * j + 1)
                    wait_bank("attn", j, "qa")
                    wait_bank("attn", j, "qb")
                for h in heads:
                    bank = free_bank("attn", j, f"s{h}")
                    a = HD * (h % 2)
                    q, k = qT[a:a + HD, h // 2, :], kT_j[a:a + HD, :]
                    pe.matmul(spare[:, bank, 0:P], q[:, 0:P], k[:, 0:P], start=True, stop=True)
                    pe.matmul(spare[:, bank, P:3 * P], q[:, P:SEQ], k, start=True, stop=True
                              ).then_inc(bank_in[bank], 1)

            def turn_probs(j, heads):
                for h in heads:
                    pe.wait_ge(prob, j * QPK + h + 1)
                    bank = free_bank("attn", j, f"p{h}")
                    for b in range(3):
                        last = turn(bank, b * P, s_sb[:, h, b * P:(b + 1) * P])
                    last.then_inc(bank_in[bank], 1)

            def weighted(j):
                pe.wait_ge(kv_copy, 2 * j + 2)
                for h in range(QPK - 4, QPK):
                    wait_bank("attn", j, f"p{h}")
                bank = free_bank("attn", j, "o0")
                for h in range(QPK):
                    last = pe.matmul(spare[:, bank, h * HD:(h + 1) * HD], pT[:, h, 0:P], v_j[:, 0, :],
                                     start=True, stop=True)
                last.then_inc(bank_in[bank], 1)
                bank = free_bank("attn", j, "o1")
                for h in range(QPK):
                    to = spare[:, bank, h * HD:(h + 1) * HD]
                    pe.matmul(to, pT[:, h, P:2 * P], v_j[:, 0, :], start=True, stop=False)
                    last = pe.matmul(to, pT[:, h, 2 * P:3 * P], v_j[:, 1, :], start=False, stop=True)
                last.then_inc(bank_in[bank], 1)

            def attn_tail(j, at):
                if at == 0:
                    scores(j, (4, 5))
                if at == 1:
                    scores(j, (6, 7))
                if 5 <= at <= 8:
                    turn_probs(j, (2 * (at - 5), 2 * (at - 5) + 1))
                if at == 10:
                    weighted(j)
                if at == 13:
                    wait_bank("attn", j, "o0")
                    wait_bank("attn", j, "o1")
                    turn_rows("attn", j, ("oa", "ob"), o_tok)

            def attn(j, first):
                for l in range(16):
                    if first and l == 1:
                        pe.wait_ge(k_rotated, 1)
                        for b, what in enumerate(("ka", "kb")):
                            bank = free_bank("prep", 0, what)
                            for k in range(2):
                                for t in range(TOK):
                                    src = k_rot[:, t, 2 * b + k, :, :].rearrange("p a d -> p (a d)")
                                    last = turn(bank, k * SEQ + t * P, src)
                            last.then_inc(bank_in[bank], 1)
                    if first and l == 2:
                        pair, use = acc_use("kvdt", 0, 1)
                        pe.wait_ge(acc_out[pair], use + 1)
                        bank = free_bank("prep", 0, "raw")
                        for t in range(TOK):
                            last = turn(bank, t * HEADS, rows_sb[:, t * P:(t + 1) * P], HEADS)
                        last.then_inc(bank_in[bank], 1)
                    if first and l == 8:
                        decays_cumulated()
                    if not first:
                        attn_tail(j - 1, l)
                    if l == 12:
                        pe.wait_ge(q_rotated, j + 1)
                        turn_rows("attn", j, ("qa", "qb"), q_rot)
                    if l == 14:
                        scores(j, (0, 1))
                    if l == 15:
                        scores(j, (2, 3))
                    slab("attn", j, l // 8, l % 8, a_hi, a_lo)

            def decays_cumulated():
                pe.wait_ge(dec_v, 3)
                pe.wait_ge(setup, 1)
                adt = spl[:, 5, :].rearrange("p (t h) -> p t h", t=TOK)
                bank = free_bank("prep", 0, "acs")
                for t in range(TOK):
                    pe.matmul(spare[:, bank, t * HEADS:(t + 1) * HEADS], upper[:, :], adt[:, t, :],
                              start=True, stop=True)
                pe.matmul(spare[:, bank, 2 * HEADS:3 * HEADS], ones[:, :], adt[:, 0, :], start=True, stop=True
                          ).then_inc(bank_in[bank], 1)
                bank = free_bank("prep", 0, "rows")
                for t in range(TOK):
                    last = pe.matmul(spare[0:HEADS, bank, t * P:(t + 1) * P], adt[:, t, :], upper[:, :],
                                     start=True, stop=True)
                last.then_inc(bank_in[bank], 1)

            attn(0, True)
            with pe.Fori(1, KVH) as j:
                attn(j, False)
            wait_bank("attn", KVH - 2, "oa")
            wait_bank("attn", KVH - 2, "ob")
            for j in range(2):
                for l, (c, k) in enumerate(ATTN_O_ORDER[j]):
                    for at in LAST_UNIT[l] if j == 0 else ():
                        attn_tail(KVH - 1, at)
                    if j == 0 and l == 12:
                        wait_bank("attn", KVH - 1, "oa")
                        wait_bank("attn", KVH - 1, "ob")
                    slab("attn_o", j, c, k, o_hi, o_lo, at=l)

            def ssd_tail(g, at):
                if at == 1:
                    pe.wait_ge(silu_bc, g + 1)
                    bank = free_bank("ssd", g, "cb")
                    turn(bank, 0, bcT[:, 0, 0:P])
                    for t in range(TOK):
                        last = pe.matmul(spare[:, bank, (1 + t) * P:(2 + t) * P], bcT[:, 0, t * P:(t + 1) * P],
                                         bcT[:, 1, t * P:(t + 1) * P], start=True, stop=True)
                    last.then_inc(bank_in[bank], 1)
                if at == 5:
                    pe.wait_ge(b_out, g + 1)
                    pe.wait_ge(weighed, 2 * g + 1)
                    bank = free_bank("ssd", g, "st")
                    pe.matmul(spare[:, bank, :], b_tok[:, :], x_end[:, :], start=True, stop=True
                              ).then_inc(bank_in[bank], 1)
                if at in (6, 7):
                    t = at - 6
                    pe.wait_ge(mixed, 2 * g + 1 + t)
                    bank = free_bank("ssd", g, f"y{t}")
                    for h in range(HPG):
                        last = pe.matmul(spare[:, bank, h * HD:(h + 1) * HD], seg_of(g)[:, h, t * P:(t + 1) * P],
                                         xs[:, t, h * HD:(h + 1) * HD], start=True, stop=True)
                    last.then_inc(bank_in[bank], 1)
                if at == 8:
                    wait_bank("ssd", g, "st")
                    bank = free_bank("ssd", g, "yoff")
                    pe.matmul(spare[:, bank, :], bcT[:, 1, P:SEQ], state[:, :], start=True, stop=True
                              ).then_inc(bank_in[bank], 1)
                if at == 16:
                    pe.wait_ge(scaled, g + 1)
                    turn_rows("ssd", g, ("ya", "yb"), sz)

            slot = [0]

            def seg_of(_):
                return seg[:, slot[0], :, :]

            def taken(i, c):
                pair, use = acc_use("ssd", i, c)
                pe.wait_ge(acc_out[pair], use + 1)

            def ssd(i, first):
                for s in range(2):
                    g = i * 2 + s
                    for l in range(24):
                        if not (first and s == 0):
                            slot[0] = 1 - s
                            ssd_tail(g - 1, l)
                        if l == 10:
                            taken(i, 3 * s)
                            turn_rows("ssd", g, ("xa", "xb"), u_tok)
                        if l == 20:
                            taken(i, 3 * s + 1)
                            bank = free_bank("ssd", g, "bc")
                            for k in range(2):
                                for t in range(TOK):
                                    last = turn(bank, k * SEQ + t * P, u_tok[:, t, k * P:(k + 1) * P])
                            last.then_inc(bank_in[bank], 1)
                        if l == 22:
                            pe.wait_ge(silu_x, g + 1)
                            for t in range(TOK):
                                bank = free_bank("ssd", g, f"x{t}")
                                for k in range(TPG):
                                    last = turn(bank, k * P, conv[:, k, t * P:(t + 1) * P])
                                last.then_inc(bank_in[bank], 1)
                        c = 3 * s + l // 8
                        slab("ssd", i, c, l % 8, a_hi, a_lo, 2 * NS if c % 3 == 1 else W)

            ssd(0, True)
            with pe.Fori(1, GROUPS // 2) as i:
                ssd(i, False)

            def merge_turn(u):
                pe.wait_ge(gated, GROUPS + u + 1)
                turn_rows("merge", u, ("ma", "mb"), sz)

            def merge(i, first):
                for l in range(24):
                    if first:
                        slot[0] = 1
                        ssd_tail(GROUPS - 1, l)
                        if l == 22:
                            wait_bank("ssd", GROUPS - 1, "ya")
                            wait_bank("ssd", GROUPS - 1, "yb")
                    elif l == 4:
                        merge_turn(i - 1)
                    if l < 8:
                        slab("merge", i, 0, l, a_hi, a_lo)
                    else:
                        slab("merge", i, 1, l - 8, y_hi, y_lo)

            merge(0, True)
            with pe.Fori(1, NC_D) as i:
                merge(i, False)
            for l in range(32):
                if l == 4:
                    merge_turn(NC_D - 1)
                if l == 6:
                    wait_bank("merge", NC_D - 1, "ma")
                    wait_bank("merge", NC_D - 1, "mb")
                if l == 0:
                    wait_bank("merge", NC_D - 2, "mb")
                slab("out", 0, l // 8, l % 8, o_hi, o_lo)
            ffn(2, "ln2", NC_D)

        @block.scalar
        def _(act):
            ch = Chain(act, s_seq)

            def split(phase, i, l, width=W):
                n = slab_no(phase, i, l)
                act.wait_ge(landed[l % LAND], loads(phase, i, l) * 16)
                if not (isinstance(n, int) and n < SPLIT):
                    act.wait_ge(used, n - SPLIT + 1)
                act.activation(w_hi[:, l % SPLIT, :, 0:width], land[:, l % LAND, :, 0:width], ACT.Copy
                               ).then_inc(high, 1)

            def bank_ready(phase, u, what):
                bank, use = spare_use(phase, u, what)
                act.wait_ge(bank_in[bank], use + 1)
                return bank

            def read_bank(phase, u, what):
                bank, use = spare_use(phase, u, what)
                act.wait_ge(bank_out[bank], use + 1)

            def acc_ready(phase, i, c):
                chunks = PHASES[phase][1]
                act.wait_ge(used, slab_no(phase, i, sum(n for n, _ in chunks[:c + 1]) - 1) + 1)
                pair = chunks[c][1]
                return pair, acc[:, 2 * pair:2 * pair + 2, :]

            def two_tiles(bank):
                return spare[:, bank, :].rearrange("p (k n) -> p k n", k=2)

            def high_tiles(phase, u, names, dst, k0, scale=1.0):
                for b, what in enumerate(names):
                    bank = bank_ready(phase, u, what)
                    act.activation(dst[:, bass.ds(k0 + 2 * b, 2), :], two_tiles(bank), ACT.Copy, scale=scale
                                   ).then_inc(tile_hi, 1)

            def ln_tile(phase, u, cols):
                bank = bank_ready(phase, 0, f"t{u}")
                if cols is None:
                    act.activation(a_hi[:, 2 * u:2 * u + 2, :], two_tiles(bank), ACT.Copy).then_inc(tile_hi, 1)
                    return
                for k in range(2):
                    last = act.activation(a_hi[:, 2 * u + k, :], two_tiles(bank)[:, k, :], ACT.Identity,
                                          scale=ln_col[:, cols, 2 * u + k:2 * u + k + 1],
                                          bias=ln_col[:, cols + 1, 2 * u + k:2 * u + k + 1])
                last.then_inc(tile_hi, 1)

            def sines():
                act.wait_ge(setup, 1)
                act.wait_ge(trig, 1)
                ch.link(act.activation(ang[:, 5, :], ang[:, 4, :], ACT.Abs))
                flat = "p t n -> p (t n)"
                act.activation(sinr[:, :, :].rearrange(flat), ang[:, 4, :], ACT.Sin)
                act.activation(cosr[:, :, :].rearrange(flat), ang[:, 5, :], ACT.Sin, scale=-1.0, bias=half_pi[:, :]
                               ).then_inc(trig_s, 1)

            def up(phase, i, first, ln, cols):
                for l in range(16):
                    if first and l < 8:
                        ln_tile(ln, l, cols)
                    if phase == "up1" and first and l == 12:
                        sines()
                    if not first and l == 6:
                        high_tiles(phase, i - 1, ("ga", "gb"), g_hi, (i - 1) * 4)
                    if l == 10:
                        pair, gate = acc_ready(phase, i, 0)
                        _, use = acc_use(phase, i, 1)
                        if not (isinstance(use, int) and use == 0):
                            act.wait_ge(acc_out[1], use)
                        if phase == "up2" and first:
                            act.wait_ge(kept_out, 2 * 16 * NC_D)
                        act.activation(silu_t, gate, ACT.Silu).then_inc(acc_out[pair], 1)
                    if not (phase == "up2" and first and l < EARLY):
                        split(phase, i, l)

            def ffn(f, ln, cols):
                phase = f"up{f}"
                up(phase, 0, True, ln, cols)
                with act.Fori(1, NC_F) as i:
                    up(phase, i, False, ln, cols)
                for j in range(2):
                    for l in range(44):
                        if j == 0 and l == 6:
                            high_tiles(phase, NC_F - 1, ("ga", "gb"), g_hi, (NC_F - 1) * 4)
                        split(f"down{f}", j, l)

            ffn(1, "xT", None)
            for l in range(EARLY):
                split("kvdt", 0, l)
            act.wait_ge(used, slab_no("down1", 1, 43) + 1)
            for k, src in enumerate((dt_bias, a_log, d_skip)):
                act.dma_start(head_r[:, k, :], src[0].partition_broadcast(P)).then_inc(row_in, 16)
            for l in range(16):
                if l < 8:
                    ln_tile("ln1", l, 0)
                if l == 11:
                    _, kv = acc_ready("kvdt", 0, 0)
                    act.activation(v_all[:, :, :], kv[:, :, KVH * HD:], ACT.Copy).then_inc(v_kept, 1)
                if l >= EARLY:
                    split("kvdt", 0, l, W if l < 8 else HEADS)

            def exp_head(j, h):
                act.wait_ge(maxed, 2 * j + h // 4 + 1)
                if h % 4 == 0:
                    act.activation(soft[:, 32 + 2 * h:40 + 2 * h], soft[:, 32 + 2 * h:40 + 2 * h], ACT.Exp)
                for b, (c0, c1) in enumerate(((0, P), (P, 3 * P))):
                    col = 2 * h + b
                    last = act.activation(s_sb[:, h, c0:c1], s_sb[:, h, c0:c1], ACT.Exp,
                                          bias=soft[:, 16 + col:17 + col], accum_out=soft[:, 48 + col:49 + col])
                last.then_inc(prob, 1)

            def attn_tail(j, at):
                if at == 2:
                    pair, gate = acc_ready("attn", j, 1)
                    act.activation(gate_a[:, :, bass.ds(j * W, W)], gate, ACT.Tanh, scale=0.5
                                   ).then_inc(acc_out[pair], 1)
                if 5 <= at <= 8:
                    exp_head(j, 2 * (at - 5))
                    exp_head(j, 2 * (at - 5) + 1)
                if at == 14:
                    high_tiles("attn", j, ("oa", "ob"), o_hi, j * 4)

            def attn(j, first):
                for l in range(16):
                    if not first:
                        attn_tail(j - 1, l)
                    if first and l == 2:
                        pair, steps = acc_ready("kvdt", 0, 1)
                        act.activation(rows_sb[:, :], steps[0:HEADS, 0, 0:SEQ], ACT.Copy).then_inc(acc_out[pair], 1)
                    if first and l == 7:
                        act.wait_ge(dec_v, 2)
                        act.wait_ge(row_in, 48)
                        act.activation(spl[:, 2, :], spl[:, 1, :], ACT.Exp)
                        act.activation(head_r[:, 1, :], head_r[:, 1, :], ACT.Exp).then_inc(dec_s, 1)
                    if first and l == 3:
                        for b, what in enumerate(("ka", "kb")):
                            bank = bank_ready("prep", 0, what)
                            act.activation(kT[:, 2 * b:2 * b + 2, :], two_tiles(bank), ACT.Copy
                                           ).then_inc(bank_out[bank], 1)
                    if first and l == 12:
                        bank = bank_ready("prep", 0, "rows")
                        act.activation(rows_sb[:, :], spare[0:HEADS, bank, 0:SEQ], ACT.Copy
                                       ).then_inc(bank_out[bank], 1)
                        _, use = spare_use("prep", 0, "rows")
                        act.wait_ge(bank_out[bank], use + 1)
                        act.dma_start(acs_rows, rows_sb[:, :]).then_inc(rows_out, 16)
                    if first and l == 13:
                        act.wait_ge(dec_v, 3)
                        _, use = spare_use("prep", 0, "acs")
                        act.wait_ge(bank_out[2], use + 1)
                        act.activation(spl[:, 0, 0:HEADS], spl[:, 0, 0:HEADS], ACT.Exp)
                        act.activation(vec_d[:, :, 5, :], vec_d[:, :, 1, :], ACT.Exp).then_inc(dec_s, 1)
                    if l == 13:
                        for b, what in enumerate(("qa", "qb")):
                            bank = bank_ready("attn", j, what)
                            act.activation(qT[:, 2 * b:2 * b + 2, :], two_tiles(bank), ACT.Copy
                                           ).then_inc(bank_out[bank], 1)
                    split("attn", j, l)

            attn(0, True)
            act.wait_ge(kept_out, 16 * NC_D)
            with act.Fori(1, KVH) as j:
                attn(j, False)
            for j in range(2):
                for l in range(16):
                    for at in LAST_UNIT[l] if j == 0 else ():
                        attn_tail(KVH - 1, at)
                    split("attn_o", j, l)

            def silu_z(i, c, g):
                pair, z = acc_ready("ssd", i, c)
                bank, use = spare_use("ssd", g - 1, "yb")
                act.wait_ge(bank_in[bank], use + 1)
                act.activation(sz[:, :, :], z, ACT.Silu).then_inc(acc_out[pair], 1)

            def ssd_tail(i, s, g, at):
                if at == 0:
                    for t in range(TOK):
                        bank = bank_ready("ssd", g, f"x{t}")
                        act.activation(xs[:, t, :], spare[:, bank, :], ACT.Copy).then_inc(bank_out[bank], 1)
                if at == 5:
                    bank = bank_ready("ssd", g, "cb")
                    act.activation(b_tok[:, :], spare[:, bank, 0:P], ACT.Copy).then_inc(b_out, 1)
                if at == 1:
                    read_bank("ssd", g, "bc")
                    act.activation(bcT[:, :, :], bcT[:, :, :], ACT.Silu).then_inc(silu_bc, 1)
                if at == 3:
                    silu_z(i, 3 * s + 2, g)
                if at == 9:
                    bank = bank_ready("ssd", g, "st")
                    act.activation(state[:, :], spare[:, bank, :], ACT.Copy).then_inc(bank_out[bank], 1)
                if at == 14:
                    act.wait_ge(gated, g + 1)
                    for t, scrap in enumerate((x_end, state)):
                        last = act.activation(scrap[:, :], sz[:, t, :], ACT.Square, scale=W ** -0.5,
                                              accum_out=rms[:, t:t + 1])
                    last.then_inc(squared, 1)
                if at == 16:
                    act.wait_ge(rms_p, g + 1)
                    for t in range(TOK):
                        last = act.activation(sz[:, t, :], sz[:, t, :], ACT.Copy, scale=rms[:, t:t + 1])
                    last.then_inc(scaled, 1)
                if at == 18:
                    for b, what in enumerate(("ya", "yb")):
                        bank = bank_ready("ssd", g, what)
                        for k in range(2):
                            ct = 2 * b + k
                            last = act.activation(y_hi[:, bass.ds(g * TPG + ct, 1), :], two_tiles(bank)[:, k:k + 1, :],
                                                  ACT.Copy, scale=grp_c[:, s, 30 + ct:31 + ct])
                        last.then_inc(tile_hi, 1)

            def first_taps(s, bank, dst, at):
                for k in range(2):
                    c = at + 5 * k
                    last = act.activation(dst[:, k, :], two_tiles(bank)[:, k, :], ACT.Identity,
                                          scale=grp_c[:, s, c + CONV - 1:c + CONV],
                                          bias=grp_c[:, s, c + CONV:c + CONV + 1])
                last.then_inc(taps, 1)

            def ssd(i, first):
                for s in range(2):
                    g = i * 2 + s
                    for l in range(24):
                        if not (first and s == 0):
                            ssd_tail(i - 1 + s, 1 - s, g - 1, l)
                        if l in (6, 7):
                            t = l - 6
                            act.wait_ge(args, 2 * g + t + 1)
                            view = seg[:, s, :, t * P:(t + 1) * P]
                            act.activation(view, view, ACT.Exp).then_inc(exps, 1)
                        if l == 11:
                            pair, x_acc = acc_ready("ssd", i, 3 * s)
                            if not (first and s == 0):
                                bank_ready("ssd", g - 1, "bc")
                            act.activation(u_tok[:, :, :], x_acc, ACT.Copy).then_inc(acc_out[pair], 1)
                        if l in (16, 17):
                            b = l - 16
                            first_taps(s, bank_ready("ssd", g, "xa" if b == 0 else "xb"),
                                       conv[:, 2 * b:2 * b + 2, :], 10 * b)
                        if l == 20:
                            pair, bc = acc_ready("ssd", i, 3 * s + 1)
                            bank_ready("ssd", g, "xb")
                            act.activation(u_tok[:, :, 0:2 * NS], bc[:, :, 0:2 * NS], ACT.Copy
                                           ).then_inc(acc_out[pair], 1)
                        if l == 22:
                            read_bank("ssd", g, "xa")
                            read_bank("ssd", g, "xb")
                            act.activation(conv[:, :, :], conv[:, :, :], ACT.Silu).then_inc(silu_x, 1)
                        if l == 23:
                            first_taps(s, bank_ready("ssd", g, "bc"), bcT, 20)
                        split("ssd", i, s * 24 + l, W if l // 8 != 1 else 2 * NS)

            ssd(0, True)
            with act.Fori(1, GROUPS // 2) as i:
                ssd(i, False)

            def merge_high(u):
                high_tiles("merge", u, ("ma", "mb"), o_hi, u * 4, 0.5)

            def merge(i, first):
                for l in range(24):
                    if first:
                        ssd_tail(GROUPS // 2 - 1, 1, GROUPS - 1, l)
                    elif l == 6:
                        merge_high(i - 1)
                    if l == 19:
                        pair, gate = acc_ready("merge", i, 0)
                        if first:
                            bank_ready("ssd", GROUPS - 1, "yb")
                        else:
                            bank_ready("merge", i - 1, "mb")
                        act.activation(sz[:, :, :], gate, ACT.Tanh, scale=0.5).then_inc(acc_out[pair], 1)
                    split("merge", i, l)

            merge(0, True)
            with act.Fori(1, NC_D) as i:
                merge(i, False)
            for l in range(32):
                if l == 5:
                    merge_high(NC_D - 1)
                split("out", 0, l)
            for l in range(EARLY):
                split("up2", 0, l)
            ffn(2, "ln2", 2)
            act.wait_ge(ln_x, 2 * NC_D + 1)
            for c in range(NC_D):
                for t in range(TOK):
                    part = resid[:, t, c * W:(c + 1) * W]
                    last = act.activation(part, part, ACT.Identity, scale=rstd[:, t:t + 1], bias=shift[:, t:t + 1])
                last.then_inc(normed, 1)
            for c in (0, 2, 1, 3):
                if c < POOL_BIASES:
                    act.wait_ge(biased, c + 1)
                else:
                    act.wait_ge(ln_x, 2 * NC_D + 2 + c - POOL_BIASES)
                act.dma_start(out_view[:, :, c * W:(c + 1) * W], resid[:, :, c * W:(c + 1) * W]).then_inc(stored, 16)

        @block.vector
        def _(dve):
            ch = Chain(dve, v_seq)

            def split(phase, i, l, width=W):
                dve.wait_ge(high, slab_no(phase, i, l) + 1)
                dve.tensor_tensor(w_lo[:, l % SPLIT, :, 0:width], land[:, l % LAND, :, 0:width],
                                  w_hi[:, l % SPLIT, :, 0:width].bitcast(F32), ALU.subtract).then_inc(rest, 1)

            def bank_ready(phase, u, what):
                bank, use = spare_use(phase, u, what)
                dve.wait_ge(bank_in[bank], use + 1)
                return bank

            def read_done(phase, u, what):
                bank, use = spare_use(phase, u, what)
                dve.wait_ge(bank_out[bank], use + 1)

            def acc_ready(phase, i, c):
                chunks = PHASES[phase][1]
                dve.wait_ge(used, slab_no(phase, i, sum(n for n, _ in chunks[:c + 1]) - 1) + 1)
                pair = chunks[c][1]
                return pair, acc[:, 2 * pair:2 * pair + 2, :]

            def two_tiles(bank):
                return spare[:, bank, :].rearrange("p (k n) -> p k n", k=2)

            def rest_tiles(phase, u, names, hi, lo, k0, scale=1.0):
                for b, what in enumerate(names):
                    bank = bank_ready(phase, u, what)
                    dve.wait_ge(tile_hi, high_no(phase, u, what) + 1)
                    at = bass.ds(k0 + 2 * b, 2)
                    dve.scalar_tensor_tensor(out=lo[:, at, :], in0=two_tiles(bank), scalar=scale,
                                             in1=hi[:, at, :].bitcast(F32), op0=ALU.mult, op1=ALU.subtract
                                             ).then_inc(bank_out[bank], 1)

            def ln_tile(phase, u, cols):
                what = f"t{u}"
                bank = bank_ready(phase, 0, what)
                at = slice(2 * u, 2 * u + 2)
                dve.wait_ge(tile_hi, high_no(phase, 0, what) + 1)
                if cols is None:
                    dve.tensor_tensor(a_lo[:, at, :], two_tiles(bank), a_hi[:, at, :].bitcast(F32), ALU.subtract
                                      ).then_inc(bank_out[bank], 1)
                    return
                h = sz[:, u % 2, :].rearrange("p (k n) -> p k n", k=2)
                for k in range(2):
                    last = dve.tensor_scalar(h[:, k, :], two_tiles(bank)[:, k, :],
                                             ln_col[:, cols, 2 * u + k:2 * u + k + 1],
                                             ln_col[:, cols + 1, 2 * u + k:2 * u + k + 1], ALU.mult, ALU.add)
                ch.link(last)
                dve.tensor_tensor(a_lo[:, at, :], h, a_hi[:, at, :].bitcast(F32), ALU.subtract
                                  ).then_inc(bank_out[bank], 1)

            def statistics(c):
                for t in range(TOK):
                    last = dve.bn_stats(stats[:, t, c, :] if isinstance(c, int) else
                                        stats[:, t, bass.ds(c, 1), :].rearrange("p a n -> p (a n)"),
                                        resid[:, t, bass.ds(c * W, W)])
                return last

            def evacuate(phase, i, cc, c, scale):
                pair, product = acc_ready(phase, i, cc)
                part = resid[:, :, bass.ds(c * W, W)]
                dve.scalar_tensor_tensor(out=part, in0=product, scalar=scale, in1=part, op0=ALU.mult, op1=ALU.add
                                         ).then_inc(acc_out[pair], 1)
                _, use = acc_use(phase, i, cc)
                dve.wait_ge(acc_out[pair], use + 1)
                ch.link(statistics(c))

            def prepare_rows(fills, c):
                part = resid[:, :, bass.ds(c * W, W)]
                dve.wait_ge(resid_in, (fills + 1) * 16)
                dve.wait_ge(rows_in, fills * 32)
                gain, bias = (rows[:, k:k + 1, bass.ds(c * W, W)].to_broadcast([P, TOK, W]) for k in range(2))
                ch.link(dve.scalar_tensor_tensor(out=part, in0=part, scalar=ALPHA, in1=gain, op0=ALU.mult,
                                                 op1=ALU.mult))
                ch.link(dve.scalar_tensor_tensor(out=part, in0=bias, scalar=ALPHA, in1=part, op0=ALU.mult,
                                                 op1=ALU.add))

            def normalise(no):
                for t in range(TOK):
                    last = dve.bn_aggr(mv[:, t, :], stats[:, t, :, :].rearrange("p c n -> p (c n)"))
                last.then_inc(ln_v, 1)
                dve.wait_ge(ln_p, no)

            def ln_chunk(c):
                for t in range(TOK):
                    part = resid[:, t, c * W:(c + 1) * W]
                    last = dve.tensor_scalar(part, part, mv[:, t, 0:1], rstd[:, t:t + 1], ALU.subtract, ALU.mult)
                last.then_inc(ln_x, 1)

            def product(phase, i):
                pair, use = acc_use(phase, i, 0)
                dve.wait_ge(acc_out[pair], use + 1)
                pair, upper_half = acc_ready(phase, i, 1)
                if not (isinstance(i, int) and i == 0):
                    bank_ready(phase, i - 1, "gb")
                dve.tensor_tensor(prod, silu_t, upper_half, ALU.mult).then_inc(acc_out[pair], 1)

            def up(phase, i, first, ln, cols):
                for l in range(16):
                    if first and l < 8:
                        ln_tile(ln, l, cols)
                        if cols is not None and l in (0, 1):
                            ln_chunk(l + 2)
                    if not first and l == 2:
                        product_of(phase, i)
                    if not first and l == 7:
                        rest_tiles(phase, i - 1, ("ga", "gb"), g_hi, g_lo, (i - 1) * 4)
                    if phase == "up1" and first and l == 7:
                        columns()
                    if phase == "up1" and first and l == 9:
                        angles()
                    if not (phase == "up2" and first and l < EARLY):
                        split(phase, i, l)

            def product_of(phase, i):
                product(phase, i - 1)

            def down(f):
                phase = f"down{f}"
                for j in range(2):
                    for l in range(44):
                        if j == 0 and l == 3:
                            product(f"up{f}", NC_F - 1)
                        if j == 0 and l == 7:
                            rest_tiles(f"up{f}", NC_F - 1, ("ga", "gb"), g_hi, g_lo, (NC_F - 1) * 4)
                        if l in (18, 36):
                            c = 2 * j + l // 36
                            if f == 1:
                                part = resid[:, :, c * W:(c + 1) * W]
                                dve.wait_ge(resid_in, 16)
                                ch.link(dve.tensor_scalar(part, part, ALPHA, None, ALU.mult))
                            else:
                                prepare_rows(2, c)
                        if l == 25:
                            evacuate(phase, j, 0, 2 * j, 0.5)
                        if j == 1 and l == 3:
                            evacuate(phase, 0, 1, 1, 0.5)
                        split(phase, j, l)
                for l in range(EARLY if f == 1 else 0):
                    split("kvdt", 0, l)
                evacuate(phase, 1, 1, 3, 0.5)

            def ffn(f, ln, cols):
                phase = f"up{f}"
                up(phase, 0, True, ln, cols)
                with dve.Fori(1, NC_F) as i:
                    up(phase, i, False, ln, cols)
                down(f)

            def columns():
                dve.wait_ge(par_t, 1)
                col = acc[:, 2, :]
                for j in range(CONV + 1):
                    at = [0, KX, P, P + KX, 2 * P][j]
                    dve.tensor_copy(vec_c[:, :, 0:20].rearrange("p g (c j) -> p g c j", j=5)[:, :, :, j],
                                    col[:, at:at + KI].rearrange("p (g c) -> p g c", c=TPG))
                    dve.tensor_copy(vec_c[:, :, 20:30].rearrange("p g (c j) -> p g c j", j=5)[:, :, :, j],
                                    col[:, at + KI:at + KX].rearrange("p (c g) -> p g c", c=2))
                dve.tensor_copy(vec_c[:, :, 30:34],
                                col[:, 2 * P + KX:2 * P + KX + KI].rearrange("p (g c) -> p g c", c=TPG))
                dve.tensor_copy(ln_col[:, :, :], col[:, 3 * P:3 * P + 4 * KD].rearrange("p (a k) -> p a k", a=4)
                                ).then_inc(dec_v, 1)

            def angles():
                a, b, c = two_pi_parts()
                magic = 1.5 * 2.0 ** 23
                big = 1024.0
                dve.wait_ge(pos_in, 16 * (TOK + 1))
                dve.wait_ge(setup, 1)
                ch.link(dve.tensor_copy(pos_f[:, :], pos_i[:, :]))
                angle, n, hi, lo, r = (ang[:, k, :] for k in range(5))
                ch.link(dve.tensor_tensor(angle.rearrange("p (t n) -> p t n", t=TOK),
                                          pos_f[:, :].unsqueeze(2).to_broadcast([P, TOK, HALF]),
                                          inv_f[:, :].unsqueeze(1).to_broadcast([P, TOK, HALF]), ALU.mult))

                def whole(src, scale):
                    ch.link(dve.tensor_scalar(n, src, scale, magic, ALU.mult, ALU.add))
                    ch.link(dve.tensor_scalar(n, n, magic, None, ALU.subtract))

                def less(dst, src, part):
                    ch.link(dve.scalar_tensor_tensor(out=dst, in0=n, scalar=-part, in1=src, op0=ALU.mult, op1=ALU.add))

                whole(angle, float(1.0 / (2 * np.pi * big)))
                less(hi, angle, a * big)
                less(hi, hi, b * big)
                ch.link(dve.tensor_scalar(lo, n, -c * big, None, ALU.mult))
                whole(hi, float(1.0 / (2 * np.pi)))
                less(hi, hi, a)
                less(hi, hi, b)
                ch.link(dve.tensor_tensor(hi, hi, lo, ALU.add))
                less(r, hi, c)
                pi = float(np.nextafter(np.float32(np.pi), np.float32(0)))
                dve.tensor_scalar(r, r, pi, -pi, ALU.min, ALU.max).then_inc(trig, 1)

            ffn(1, "xT", None)

            def rotate(src, dst_lo, dst_hi, heads, signal):
                shape = [P, TOK, heads, HALF]
                cos = cosr[:, :, :].unsqueeze(2).to_broadcast(shape)
                sin = sinr[:, :, :].unsqueeze(2).to_broadcast(shape)
                u1, u2 = src[:, :, :, 0:HALF], src[:, :, :, HALF:HD]
                n = TOK * heads * HALF
                tmp = [rot[:, k, 0:n].rearrange("p (t h d) -> p t h d", t=TOK, h=heads) for k in range(4)]
                dve.tensor_tensor(tmp[0], u1, cos, ALU.mult)
                dve.tensor_tensor(tmp[1], u2, sin, ALU.mult)
                dve.tensor_tensor(tmp[2], u2, cos, ALU.mult)
                signal(dve.tensor_tensor(tmp[3], u1, sin, ALU.mult))
                for d in dst_lo:
                    dve.tensor_tensor(d, tmp[0], tmp[1], ALU.subtract)
                for d in dst_hi:
                    last = dve.tensor_tensor(d, tmp[2], tmp[3], ALU.add)
                return last

            normalise(1)
            ln_chunk(0)
            ln_chunk(1)
            for l in range(16):
                if l < 8:
                    ln_tile("ln1", l, 0)
                    if l in (0, 1):
                        ln_chunk(l + 2)
                if l == 13:
                    pair, kv = acc_ready("kvdt", 0, 0)
                    dve.wait_ge(trig_s, 1)
                    dve.wait_ge(v_kept, 1)

                    def free_kv(ins):
                        ins.then_inc(acc_out[0], 1)
                        dve.wait_ge(acc_out[0], acc_use("kvdt", 0, 0)[1] + 1)

                    rotate(kv[:, :, 0:KVH * HD].rearrange("p t (h d) -> p t h d", d=HD),
                           [k_rot[:, :, :, d, 0:HALF] for d in range(2)],
                           [k_rot[:, :, :, d, HALF:HD] for d in range(2)], KVH, free_kv).then_inc(k_rotated, 1)
                if l >= EARLY:
                    split("kvdt", 0, l, W if l < 8 else HEADS)

            def time_steps(part):
                v, neg, e, s, dt, adt = (spl[:, k, :] for k in range(6))
                by_token = "p (t h) -> p t h"

                def row(k):
                    return head_r[:, k:k + 1, :].to_broadcast([P, TOK, HEADS])

                if part == 0:
                    bank = bank_ready("prep", 0, "raw")
                    dve.wait_ge(row_in, 48)
                    dve.tensor_tensor(v.rearrange(by_token, t=TOK),
                                      spare[:, bank, 0:TOK * HEADS].rearrange(by_token, t=TOK), row(0), ALU.add
                                      ).then_inc(bank_out[bank], 1)
                    read_done("prep", 0, "raw")
                    dve.scalar_tensor_tensor(out=neg, in0=v, scalar=-1.0, in1=v, op0=ALU.mult, op1=ALU.min
                                             ).then_inc(dec_v, 1)
                if part == 1:
                    dve.wait_ge(dec_s, 1)
                    ch.link(dve.tensor_scalar(s, e, 2.0, None, ALU.add))
                    ch.link(dve.reciprocal(s, s))
                    ch.link(dve.tensor_tensor(s, e, s, ALU.mult))
                    q, r = neg, e
                    ch.link(dve.tensor_tensor(q, s, s, ALU.mult))
                    ch.link(dve.tensor_scalar(r, q, 1.0 / 17, None, ALU.mult))
                    for k in range(7, 3, -1):
                        ch.link(dve.scalar_tensor_tensor(out=r, in0=r, scalar=1.0 / (2 * k + 1), in1=q,
                                                         op0=ALU.add, op1=ALU.mult))
                if part == 2:
                    q, r = neg, e
                    for k in range(3, 0, -1):
                        ch.link(dve.scalar_tensor_tensor(out=r, in0=r, scalar=1.0 / (2 * k + 1), in1=q,
                                                         op0=ALU.add, op1=ALU.mult))
                    ch.link(dve.scalar_tensor_tensor(out=r, in0=r, scalar=1.0, in1=s, op0=ALU.add, op1=ALU.mult))
                    ch.link(dve.tensor_scalar(v, v, 0.0, None, ALU.max))
                    ch.link(dve.scalar_tensor_tensor(out=dt, in0=r, scalar=2.0, in1=v, op0=ALU.mult, op1=ALU.add))
                    dve.scalar_tensor_tensor(out=adt.rearrange(by_token, t=TOK), in0=dt.rearrange(by_token, t=TOK),
                                             scalar=-1.0, in1=row(1), op0=ALU.mult, op1=ALU.mult).then_inc(dec_v, 1)
                by_group = "p (g h) -> p g h"
                if part == 3:
                    bank = bank_ready("prep", 0, "acs")
                    for t in range(TOK):
                        last = dve.tensor_copy(vec_d[:, :, t, :],
                                               spare[:, bank, t * HEADS:(t + 1) * HEADS].rearrange(by_group, h=HPG))
                        dve.tensor_copy(vec_d[:, :, 2 + t, :],
                                        dt[:, t * HEADS:(t + 1) * HEADS].rearrange(by_group, h=HPG))
                    ch.link(dve.tensor_copy(vec_d[:, :, 6, :], head_r[:, 2, :].rearrange(by_group, h=HPG)))
                    dve.tensor_tensor(v[:, 0:HEADS].rearrange(by_group, h=HPG),
                                      spare[:, bank, 2 * HEADS:3 * HEADS].rearrange(by_group, h=HPG),
                                      vec_d[:, :, 0, :], ALU.subtract).then_inc(bank_out[bank], 1)
                if part == 4:
                    dve.wait_ge(dec_s, 2)
                    dve.tensor_tensor(vec_d[:, :, 4, :], v[:, 0:HEADS].rearrange(by_group, h=HPG), vec_d[:, :, 2, :],
                                      ALU.mult).then_inc(dec_v, 1)

            def score(j, heads):
                for h in heads:
                    bank = bank_ready("attn", j, f"s{h}")
                    dve.scalar_tensor_tensor(out=s_sb[:, h, :], in0=spare[:, bank, 0:3 * P], scalar=HD ** -0.5,
                                             in1=mask[:, :], op0=ALU.mult, op1=ALU.add).then_inc(bank_out[bank], 1)

            def maxima(j, half):
                for h in range(4 * half, 4 * half + 4):
                    read_done("attn", j, f"s{h}")
                h0 = 4 * half
                mx = soft[:, 2 * h0:2 * h0 + 8].rearrange("p (h b) -> p h b", b=2)
                dve.tensor_reduce(mx[:, :, 0], s_sb[:, h0:h0 + 4, 0:P], AX.X, ALU.max)
                ch.link(dve.tensor_reduce(mx[:, :, 1], s_sb[:, h0:h0 + 4, P:3 * P], AX.X, ALU.max))
                sink = sink_r[:, bass.ds(j * QPK + h0, 4)].unsqueeze(2).to_broadcast([P, 4, 2])
                ch.link(dve.tensor_tensor(mx, mx, sink, ALU.max))
                neg = soft[:, 16 + 2 * h0:24 + 2 * h0]
                ch.link(dve.tensor_scalar(neg, soft[:, 2 * h0:2 * h0 + 8], -1.0, None, ALU.mult))
                dve.tensor_tensor(soft[:, 32 + 2 * h0:40 + 2 * h0].rearrange("p (h b) -> p h b", b=2), sink,
                                  neg.rearrange("p (h b) -> p h b", b=2), ALU.add).then_inc(maxed, 1)

            def attn_tail(j, at):
                if at < 3:
                    score(j, (2 * at + 2, 2 * at + 3))
                if at in (4, 6):
                    maxima(j, (at - 4) // 2)
                if 6 <= at <= 9:
                    for h in (2 * (at - 6), 2 * (at - 6) + 1):
                        bank = bank_ready("attn", j, f"p{h}")
                        dve.tensor_copy(pT[:, h, :], spare[:, bank, 0:3 * P]).then_inc(bank_out[bank], 1)
                if at == 11:
                    dve.wait_ge(prob, j * QPK + QPK)
                    den = soft[:, 48:64]
                    ch.link(dve.tensor_tensor(den, den, soft[:, 32:48], ALU.add))
                    ch.link(dve.reciprocal(den, den))
                    for t in range(TOK):
                        bank = bank_ready("attn", j, f"o{t}")
                        dve.tensor_tensor(o_tok[:, t, :].rearrange("p (h d) -> p h d", d=HD),
                                          spare[:, bank, :].rearrange("p (h d) -> p h d", d=HD),
                                          den.rearrange("p (h b) -> p h b", b=2)[:, :, t:t + 1].to_broadcast([P, QPK, HD]),
                                          ALU.mult).then_inc(bank_out[bank], 1)
                if at == 15:
                    rest_tiles("attn", j, ("oa", "ob"), o_hi, o_lo, j * 4)

            def attn(j, first):
                for l in range(16):
                    if first and l in (6, 8, 9, 12, 14):
                        time_steps((6, 8, 9, 12, 14).index(l))
                    if not first:
                        attn_tail(j - 1, l)
                    if l == 10:
                        pair, q = acc_ready("attn", j, 0)
                        _, use = acc_use("attn", j, 0)

                        def free_q(ins):
                            ins.then_inc(acc_out[0], 1)
                            dve.wait_ge(acc_out[0], use + 1)

                        view = q_rot[:, :, :].rearrange("p t (h d) -> p t h d", d=HD)
                        rotate(q.rearrange("p t (h d) -> p t h d", d=HD), [view[:, :, :, 0:HALF]],
                               [view[:, :, :, HALF:HD]], QPK, free_q).then_inc(q_rotated, 1)
                    if l == 15:
                        score(j, (0, 1))
                    split("attn", j, l)

            attn(0, True)
            with dve.Fori(1, KVH) as j:
                ch.enter(j, 1, ATTN_LINKS)
                attn(j, False)
                ch.leave(KVH)

            def gate_attention(j, cc):
                last = max(l for l, (c, _) in enumerate(ATTN_O_ORDER[j]) if c == cc)
                dve.wait_ge(used, slab_no("attn_o", j, last) + 1)
                pair = PHASES["attn_o"][1][cc][1]
                y_a = acc[:, 2 * pair:2 * pair + 2, :]
                part = gate_a[:, :, bass.ds((j * 2 + cc) * W, W)]
                dve.scalar_tensor_tensor(out=part, in0=part, scalar=1.0, in1=y_a, op0=ALU.add, op1=ALU.mult
                                         ).then_inc(acc_out[pair], 1)

            for j in range(2):
                for l in range(16):
                    for at in LAST_UNIT[l] if j == 0 else ():
                        attn_tail(KVH - 1, at)
                    if (j, l) == (0, 15):
                        dve.wait_ge(acc_out[1], acc_use("attn", KVH - 1, 1)[1] + 1)
                        gate_attention(0, 0)
                    if (j, l) == (1, 2):
                        gate_attention(0, 1)
                    if (j, l) == (1, 11):
                        gate_attention(1, 0)
                    split("attn_o", j, l)

            def heads_of(view, n=W):
                return view.rearrange("p (h d) -> p h d", d=HD)

            def ssd_tail(i, s, g, at):
                col = grp_d[:, s, :, :]
                if at == 0:
                    dve.wait_ge(taps, 3 * g + 3)
                    bank = bank_ready("ssd", g, "bc")
                    convolve(s, [(two_tiles(bank)[:, k, :], bcT[:, k, :], 20 + 5 * k) for k in range(2)],
                             lambda ins: ins.then_inc(bank_out[bank], 1))
                if at == 5:
                    bank = bank_ready("ssd", g, "cb")
                    dve.wait_ge(b_out, g + 1)
                    dve.tensor_tensor(cbm[:, :, :], spare[:, bank, P:3 * P].rearrange("p (t n) -> p t n", t=TOK),
                                      upper[:, :].unsqueeze(1).to_broadcast([P, TOK, P]), ALU.mult
                                      ).then_inc(bank_out[bank], 1)
                if at in (6, 7):
                    t = at - 6
                    read_done("ssd", g, "cb")
                    dve.wait_ge(exps, 2 * g + t + 1)
                    for h in range(HPG):
                        m = seg[:, s, h, t * P:(t + 1) * P]
                        last = dve.scalar_tensor_tensor(out=m, in0=m, scalar=col[:, 2 + t, h:h + 1], in1=cbm[:, t, :],
                                                        op0=ALU.mult, op1=ALU.mult)
                    last.then_inc(mixed, 1)
                if at == 11:
                    dve.wait_ge(weighed, 2 * g + 2)
                    for t in range(TOK):
                        bank = bank_ready("ssd", g, f"y{t}")
                        dve.tensor_tensor(t_tok[:, t, :], t_tok[:, t, :], spare[:, bank, :], ALU.add
                                          ).then_inc(bank_out[bank], 1)
                if at == 12:
                    bank = bank_ready("ssd", g, "yoff")
                    dve.tensor_tensor(heads_of(x_end[:, :]), heads_of(spare[:, bank, :]),
                                      col[:, 5, :].unsqueeze(2).to_broadcast([P, HPG, HD]), ALU.mult
                                      ).then_inc(bank_out[bank], 1)
                    read_done("ssd", g, "yoff")
                    read_done("ssd", g, "y1")
                    ch.link(dve.tensor_tensor(t_tok[:, 1, :], t_tok[:, 1, :], x_end[:, :], ALU.add))
                if at == 13:
                    pair, use = acc_use("ssd", i, 3 * s + 2)
                    dve.wait_ge(acc_out[pair], use + 1)
                    dve.tensor_tensor(sz[:, :, :], t_tok[:, :, :], sz[:, :, :], ALU.mult).then_inc(gated, 1)
                if at == 19:
                    for b, what in enumerate(("ya", "yb")):
                        bank = bank_ready("ssd", g, what)
                        dve.wait_ge(tile_hi, high_no("ssd", g, what) + 1)
                        for k in range(2):
                            ct = 2 * b + k
                            tile = bass.ds(g * TPG + ct, 1)
                            last = dve.scalar_tensor_tensor(out=y_lo[:, tile, :], in0=two_tiles(bank)[:, k:k + 1, :],
                                                            scalar=grp_c[:, s, 30 + ct:31 + ct],
                                                            in1=y_hi[:, tile, :].bitcast(F32),
                                                            op0=ALU.mult, op1=ALU.subtract)
                        last.then_inc(bank_out[bank], 1)

            def convolve(s, jobs, signal):
                seen = [None] * len(jobs)
                for back in range(1, CONV):
                    for n, (src, dst, at) in enumerate(jobs):
                        tap = grp_c[:, s, at + CONV - 1 - back:at + CONV - back]
                        if back > 1:
                            dve.wait_ge(v_seq, seen[n])
                        ins = dve.scalar_tensor_tensor(out=dst[:, back:], in0=src[:, 0:SEQ - back], scalar=tap,
                                                       in1=dst[:, back:], op0=ALU.mult, op1=ALU.add)
                        if back < CONV - 1:
                            seen[n] = ch.mark(ins)
                        elif n == len(jobs) - 1:
                            signal(ins)

            def ssd(i, first):
                for s in range(2):
                    g = i * 2 + s
                    for l in range(24):
                        if not (first and s == 0):
                            ssd_tail(i - 1 + s, 1 - s, g - 1, l)
                        elif l == 3:
                            gate_attention(1, 1)
                        if l in (4, 5):
                            t = l - 4
                            dve.wait_ge(apart, 2 * g + t + 1)
                            m = seg[:, s, :, t * P:(t + 1) * P]
                            dve.tensor_scalar(m, m, 0.0, None, ALU.min).then_inc(args, 1)
                        if l in (18, 21):
                            b = (l - 18) // 3
                            dve.wait_ge(taps, 3 * g + b + 1)
                            bank = bank_ready("ssd", g, "xa" if b == 0 else "xb")
                            use = spare_use("ssd", g, "xa" if b == 0 else "xb")[1]

                            def done(ins, bank=bank, use=use, b=b):
                                ins.then_inc(bank_out[bank], 1)
                                if b == 1:
                                    dve.wait_ge(bank_out[bank], use + 1)

                            convolve(s, [(two_tiles(bank)[:, k, :], conv[:, 2 * b + k, :], 5 * (2 * b + k))
                                         for k in range(2)], done)
                        split("ssd", i, s * 24 + l, W if l // 8 != 1 else 2 * NS)

            ssd(0, True)
            with dve.Fori(1, GROUPS // 2) as i:
                ch.enter(i, 1, SSD_LINKS)
                ssd(i, False)
                ch.leave(GROUPS // 2)

            def merged(u):
                pair, use = acc_use("merge", u, 0)
                dve.wait_ge(acc_out[pair], use + 1)
                pair, y_s = acc_ready("merge", u, 1)
                dve.scalar_tensor_tensor(out=sz[:, :, :], in0=sz[:, :, :], scalar=1.0, in1=y_s, op0=ALU.add,
                                         op1=ALU.mult).then_inc(acc_out[pair], 1)
                _, use = acc_use("merge", u, 1)
                dve.wait_ge(acc_out[pair], use + 1)
                dve.tensor_tensor(sz[:, :, :], sz[:, :, :], gate_a[:, :, bass.ds(u * W, W)], ALU.add
                                  ).then_inc(gated, 1)

            def merge(i, first):
                for l in range(24):
                    if first:
                        ssd_tail(GROUPS // 2 - 1, 1, GROUPS - 1, l)
                    elif l == 2:
                        merged(i - 1)
                    elif l == 7:
                        rest_tiles("merge", i - 1, ("ma", "mb"), o_hi, o_lo, (i - 1) * 4, 0.5)
                    split("merge", i, l)

            merge(0, True)
            with dve.Fori(1, NC_D) as i:
                merge(i, False)
            for l in range(32):
                if l == 2:
                    merged(NC_D - 1)
                if l == 6:
                    rest_tiles("merge", NC_D - 1, ("ma", "mb"), o_hi, o_lo, (NC_D - 1) * 4, 0.5)
                if l % 8 == 7:
                    c = l // 8
                    prepare_rows(1, c)
                if l % 8 == 2 and l > 8:
                    c = l // 8 - 1
                    evacuate("out", 0, c, c, 1.0)
                split("out", 0, l)
            for l in range(EARLY):
                split("up2", 0, l)
            evacuate("out", 0, NC_D - 1, NC_D - 1, 1.0)
            normalise(2)
            ln_chunk(0)
            ln_chunk(1)
            ffn(2, "ln2", 2)
            normalise(3)
            dve.scalar_tensor_tensor(out=shift[:, :], in0=mv[:, :, 0], scalar=-1.0, in1=rstd[:, :], op0=ALU.mult,
                                     op1=ALU.mult).then_inc(ln_x, 1)
            dve.wait_ge(last_rows_in, 32)
            for c in range(NC_D):
                dve.wait_ge(normed, c + 1)
                part = resid[:, :, c * W:(c + 1) * W]
                gain, bias = (last_rows[:, k:k + 1, c * W:(c + 1) * W].to_broadcast([P, TOK, W]) for k in range(2))
                if c < POOL_BIASES:
                    dve.tensor_tensor(part, part, gain, ALU.mult).then_inc(gained, 1)
                else:
                    ch.link(dve.tensor_tensor(part, part, gain, ALU.mult))
                    dve.tensor_tensor(part, part, bias, ALU.add).then_inc(ln_x, 1)


NAMES = ["x", "positions", "ffn1_w_gate", "ffn1_w_up", "ffn1_w_down", "ln1_g", "ln1_b", "w_in", "conv_w", "conv_b",
         "dt_bias", "a_log", "d_skip", "ssd_norm_g", "w_ssd_o", "attn_sinks", "w_attn_o", "w_out", "ln2_g", "ln2_b",
         "ffn2_w_gate", "ffn2_w_up", "ffn2_w_down", "ln3_g", "ln3_b"]


def kernel(**inputs):
    import concourse.bacc as bacc
    from concourse.bass_utils import run_bass_kernel_spmd

    nc = bacc.Bacc("TRN2", target_bir_lowering=False, num_devices=1)
    arrays, args = {}, []
    for name in NAMES:
        a = np.ascontiguousarray(inputs[name])
        arrays[name] = a
        args.append(nc.dram_tensor(name, a.shape, mybir.dt.from_np(a.dtype), kind="ExternalInput").ap())
    args.append(nc.dram_tensor("acs_rows", (HEADS, SEQ), F32, kind="Internal").ap())
    args.append(nc.dram_tensor("kept", (SEQ, D), F32, kind="Internal").ap())
    args.append(nc.dram_tensor("out", (1, SEQ, D), F32, kind="ExternalOutput").ap())
    build_decoder_layer(nc, *args)
    r = run_bass_kernel_spmd(nc, [arrays], core_ids=[0])
    return r.results[0]["out"]
```
